# Optimizing a Trainium2 kernel written in Bass

```python
import math
import jax, jax.numpy as jnp
from jax import lax
import numpy as np

D_MODEL = 1024
BATCH = 1
SEQ = 256
DEPTH = 2

N_A_LAYERS = DEPTH // 2
N_B_LAYERS = DEPTH - N_A_LAYERS
S5_GROUP = 16
S5_GROUPS = D_MODEL // S5_GROUP
S5_STATE = 64
N_HEADS = 16
HEAD_DIM = D_MODEL // N_HEADS
MOBA_BLOCK = 256
MOBA_TOPK = 3
Q_CHUNK = 32
D_FF = 256 * ((8 * D_MODEL // 3 + 255) // 256)
EPS = 1e-6
NEG = -1e30

kernel_name = 'hybrid_s5_moba_macaron_yoco'

def rmsnorm(x, g):
    xf = x.astype(jnp.float32)
    xf = xf * lax.rsqrt(jnp.mean(xf * xf, axis=-1, keepdims=True) + EPS)
    return (xf * g.astype(jnp.float32)).astype(x.dtype)

def swiglu(x, w_in, w_out):
    g, u = jnp.split(x @ w_in, 2, axis=-1)
    return (jax.nn.silu(g) * u) @ w_out

def alibi_slopes():
    return jnp.exp2(-8.0 * jnp.arange(1, N_HEADS + 1, dtype=jnp.float32) / N_HEADS)

def s5_mixer(u, a_re, a_im, b_re, b_im, c_re, c_im, d_skip, log_step, w_glu):
    f32 = jnp.float32
    bsz, seq_len, _ = u.shape
    uf = u.astype(f32)
    ug = uf.reshape(bsz, seq_len, S5_GROUPS, S5_GROUP)
    dt = jnp.exp(log_step.astype(f32))[:, None]
    ar = jnp.minimum(a_re.astype(f32), -1e-4)
    ai = a_im.astype(f32)
    mag = jnp.exp(ar * dt)
    lr = mag * jnp.cos(ai * dt)
    li = mag * jnp.sin(ai * dt)
    nr = lr - 1.0
    den = ar * ar + ai * ai
    fr = (nr * ar + li * ai) / den
    fi = (li * ar - nr * ai) / den
    br = b_re.astype(f32)
    bi = b_im.astype(f32)
    bbr = fr[..., None] * br - fi[..., None] * bi
    bbi = fr[..., None] * bi + fi[..., None] * br
    bu_re = jnp.einsum('blgj,gpj->blgp', ug, bbr)
    bu_im = jnp.einsum('blgj,gpj->blgp', ug, bbi)
    a_r = jnp.broadcast_to(lr, (1, seq_len, S5_GROUPS, S5_STATE))
    a_i = jnp.broadcast_to(li, (1, seq_len, S5_GROUPS, S5_STATE))

    def combine(e1, e2):
        a1r, a1i, b1r, b1i = e1
        a2r, a2i, b2r, b2i = e2
        return (a2r * a1r - a2i * a1i,
                a2r * a1i + a2i * a1r,
                a2r * b1r - a2i * b1i + b2r,
                a2r * b1i + a2i * b1r + b2i)

    _, _, xr, xi = lax.associative_scan(combine, (a_r, a_i, bu_re, bu_im), axis=1)
    y = (jnp.einsum('blgp,gjp->blgj', xr, c_re.astype(f32))
         - jnp.einsum('blgp,gjp->blgj', xi, c_im.astype(f32)))
    y = y.reshape(bsz, seq_len, D_MODEL) + d_skip.astype(f32) * uf
    z = jax.nn.gelu(y).astype(u.dtype)
    za, zb = jnp.split(z @ w_glu, 2, axis=-1)
    return za * jax.nn.sigmoid(zb)

def shared_kv(h, kv_norm, w_kv):
    bsz, seq_len, _ = h.shape
    lp = -(-seq_len // MOBA_BLOCK) * MOBA_BLOCK
    nb = lp // MOBA_BLOCK
    kv = rmsnorm(h, kv_norm) @ w_kv
    kv = jnp.pad(kv, ((0, 0), (0, lp - seq_len), (0, 0)))
    k, v = jnp.split(kv, 2, axis=-1)

    def to_blocks(a):
        return a.reshape(bsz, nb, MOBA_BLOCK, N_HEADS, HEAD_DIM).transpose(0, 3, 1, 2, 4)

    kb = to_blocks(k)
    vb = to_blocks(v)
    kmean = jnp.mean(kb.astype(jnp.float32), axis=3).astype(kb.dtype)
    return kb, vb, kmean

def moba_attention(xn, w_q, w_o, kb, vb, kmean):
    bsz, seq_len, _ = xn.shape
    nb = kb.shape[2]
    lp = nb * MOBA_BLOCK
    n_chunks = lp // Q_CHUNK
    k_sel = min(MOBA_TOPK, nb)
    q = jnp.pad(xn @ w_q, ((0, 0), (0, lp - seq_len), (0, 0)))
    q = q.reshape(bsz, n_chunks, Q_CHUNK, N_HEADS, HEAD_DIM).transpose(1, 0, 2, 3, 4)
    starts = jnp.arange(n_chunks, dtype=jnp.int32) * Q_CHUNK
    slopes = alibi_slopes()
    scale = HEAD_DIM ** -0.5
    b_ix = jnp.arange(bsz)[:, None, None, None]
    h_ix = jnp.arange(N_HEADS)[None, None, :, None]
    offs = jnp.arange(MOBA_BLOCK, dtype=jnp.int32)

    def attend(args):
        qc, start = args
        t = start + jnp.arange(Q_CHUNK, dtype=jnp.int32)
        own = start // MOBA_BLOCK
        gate = jnp.einsum('bqhd,bhnd->bqhn', qc, kmean).astype(jnp.float32)
        gate = jnp.where(jnp.arange(nb) < own, gate, NEG)
        _, idx = lax.top_k(gate, k_sel)
        valid = jnp.arange(k_sel) < own
        kg = kb[b_ix, h_ix, idx]
        vg = vb[b_ix, h_ix, idx]
        s_sel = jnp.einsum('bqhd,bqhrkd->bqhrk', qc, kg).astype(jnp.float32) * scale
        kpos = idx[..., None] * MOBA_BLOCK + offs
        dist = (t[None, :, None, None, None] - kpos).astype(jnp.float32)
        s_sel = s_sel - slopes[None, None, :, None, None] * dist
        s_sel = jnp.where(valid[:, None], s_sel, NEG)
        k_own = lax.dynamic_index_in_dim(kb, own, axis=2, keepdims=False)
        v_own = lax.dynamic_index_in_dim(vb, own, axis=2, keepdims=False)
        s_own = jnp.einsum('bqhd,bhkd->bqhk', qc, k_own).astype(jnp.float32) * scale
        dist_own = (t[:, None] - (own * MOBA_BLOCK + offs)[None, :]).astype(jnp.float32)
        s_own = s_own - slopes[None, None, :, None] * dist_own[None, :, None, :]
        s_own = jnp.where(dist_own[None, :, None, :] >= 0, s_own, NEG)
        logits = jnp.concatenate(
            [s_sel.reshape(bsz, Q_CHUNK, N_HEADS, k_sel * MOBA_BLOCK), s_own], axis=-1)
        p = jax.nn.softmax(logits, axis=-1).astype(vb.dtype)
        p_sel = p[..., :k_sel * MOBA_BLOCK].reshape(bsz, Q_CHUNK, N_HEADS, k_sel, MOBA_BLOCK)
        p_own = p[..., k_sel * MOBA_BLOCK:]
        return (jnp.einsum('bqhrk,bqhrkd->bqhd', p_sel, vg)
                + jnp.einsum('bqhk,bhkd->bqhd', p_own, v_own))

    o = lax.map(attend, (q, starts))
    o = o.transpose(1, 0, 2, 3, 4).reshape(bsz, lp, D_MODEL)[:, :seq_len]
    return o @ w_o

def setup_inputs(seed: int = 0) -> dict:
    key = jax.random.key(seed)
    ks = jax.random.split(key, 22)
    f32 = jnp.float32
    n_a, n_b = N_A_LAYERS, N_B_LAYERS
    G, P, GC = S5_GROUPS, S5_STATE, S5_GROUP

    def nrm(k, shape, scale):
        return jax.random.normal(k, shape, f32) * scale

    def gain(k, shape):
        return 1.0 + 0.02 * jax.random.normal(k, shape, f32)

    n_idx = jnp.arange(P, dtype=f32)
    return {
        'x': jax.random.normal(ks[0], (BATCH, SEQ, D_MODEL), f32),
        'ffn1_norm': gain(ks[1], (DEPTH, D_MODEL)),
        'ffn1_w_in': nrm(ks[2], (DEPTH, D_MODEL, 2 * D_FF), D_MODEL ** -0.5),
        'ffn1_w_out': nrm(ks[3], (DEPTH, D_FF, D_MODEL), D_FF ** -0.5),
        'mix_norm': gain(ks[4], (DEPTH, D_MODEL)),
        'ffn2_norm': gain(ks[5], (DEPTH, D_MODEL)),
        'ffn2_w_in': nrm(ks[6], (DEPTH, D_MODEL, 2 * D_FF), D_MODEL ** -0.5),
        'ffn2_w_out': nrm(ks[7], (DEPTH, D_FF, D_MODEL), D_FF ** -0.5),
        's5_a_re': -0.5 + 0.01 * jax.random.normal(ks[8], (n_a, G, P), f32),
        's5_a_im': math.pi * n_idx + 0.01 * jax.random.normal(ks[9], (n_a, G, P), f32),
        's5_b_re': nrm(ks[10], (n_a, G, P, GC), (2 * GC) ** -0.5),
        's5_b_im': nrm(ks[11], (n_a, G, P, GC), (2 * GC) ** -0.5),
        's5_c_re': nrm(ks[12], (n_a, G, GC, P), P ** -0.5),
        's5_c_im': nrm(ks[13], (n_a, G, GC, P), P ** -0.5),
        's5_d': nrm(ks[14], (n_a, D_MODEL), 1.0),
        's5_log_step': jax.random.uniform(ks[15], (n_a, G), f32, math.log(1e-3), math.log(1e-1)),
        's5_w_glu': nrm(ks[16], (n_a, D_MODEL, 2 * D_MODEL), D_MODEL ** -0.5),
        'kv_norm': gain(ks[17], (D_MODEL,)),
        'w_kv': nrm(ks[18], (D_MODEL, 2 * D_MODEL), D_MODEL ** -0.5),
        'w_q': nrm(ks[19], (n_b, D_MODEL, D_MODEL), D_MODEL ** -0.5),
        'w_o': nrm(ks[20], (n_b, D_MODEL, D_MODEL), D_MODEL ** -0.5),
        'final_norm': gain(ks[21], (D_MODEL,)),
    }

def reference(x, ffn1_norm, ffn1_w_in, ffn1_w_out, mix_norm, ffn2_norm, ffn2_w_in, ffn2_w_out,
              s5_a_re, s5_a_im, s5_b_re, s5_b_im, s5_c_re, s5_c_im, s5_d, s5_log_step, s5_w_glu,
              kv_norm, w_kv, w_q, w_o, final_norm):
    h = x
    kb = vb = kmean = None
    for layer in range(DEPTH):
        if layer == N_A_LAYERS:
            kb, vb, kmean = shared_kv(h, kv_norm, w_kv)
        h = h + 0.5 * swiglu(rmsnorm(h, ffn1_norm[layer]), ffn1_w_in[layer], ffn1_w_out[layer])
        hn = rmsnorm(h, mix_norm[layer])
        if layer < N_A_LAYERS:
            h = h + s5_mixer(hn, s5_a_re[layer], s5_a_im[layer], s5_b_re[layer], s5_b_im[layer],
                             s5_c_re[layer], s5_c_im[layer], s5_d[layer], s5_log_step[layer],
                             s5_w_glu[layer])
        else:
            j = layer - N_A_LAYERS
            h = h + moba_attention(hn, w_q[j], w_o[j], kb, vb, kmean)
        h = h + 0.5 * swiglu(rmsnorm(h, ffn2_norm[layer]), ffn2_w_in[layer], ffn2_w_out[layer])
    return rmsnorm(h, final_norm)


_drawn_inputs = setup_inputs


def setup_inputs(seed=0):
    import zlib

    import numpy as np

    out = dict(_drawn_inputs(seed))
    spreads = {}
    factors = {'ffn1_norm': 4.609,
     'mix_norm': 5.778,
     'ffn2_norm': 5.108,
     's5_a_re': 8.0,
     's5_b_re': 2.77,
     's5_b_im': 2.745,
     's5_c_re': 2.786,
     's5_c_im': 2.774,
     'kv_norm': 7.363,
     'final_norm': 2.751}
    for name, (base, spread) in spreads.items():
        noise = np.random.default_rng([zlib.crc32(name.encode()), seed]).standard_normal(out[name].shape)
        drawn = base * np.exp(spread * noise) if base else spread * noise
        out[name] = __import__('jax').numpy.asarray(drawn.astype(out[name].dtype))
    for name, factor in factors.items():
        out[name] = (out[name] * factor).astype(out[name].dtype)
    return out
```

```python
import math
from contextlib import ExitStack

import concourse.bass as bass
from concourse import mybir

ALU = mybir.AluOpType
ACT = mybir.ActivationFunctionType
F32 = mybir.dt.float32
F32R = mybir.dt.float32r
AX_X = mybir.AxisListType.X

P = 128
TOK = 256
TT = TOK // P
D = 1024
DT = D // P
FF = 2816
FT = FF // P
HEADS = 16
HD = D // HEADS
EPS = 1e-6

S5_G, S5_J, S5_N = 64, 16, 64
GP = S5_G // 2
PPT = GP // DT
STEP = 4
CH = TOK // STEP

K_UNIT = 4
UW = K_UNIT * 2 * P
RAW_SLOTS = 4
SPLIT_SLOTS = 4
LEAD = 2
PAIR_BANKS = 2

NORMS = 8
SMALLS = 27
S5_LOADS = 8
BD_STEPS = 10
NEG = -1e30
ROUND = 1.5 * 2.0 ** 23
TWO_PI = (6.28125, 0.0019350051879882812, 2.0 * math.pi - 6.28125 - 0.0019350051879882812)
PI_LOW = 3.1415925

PHASES = [
    ("in", FT, DT), ("out", DT // 2, FT), ("glu", DT, DT), ("in", FT, DT), ("out", DT // 2, FT),
    ("k", DT // 2, DT), ("v", DT // 2, DT), ("in", FT, DT), ("out", DT // 2, FT),
    ("q", DT // 2, DT), ("o", DT // 2, DT), ("in", FT, DT), ("out", DT // 2, FT),
]


class Phase:

    def __init__(self, name, pairs, kt, pair0, unit0, load0, drained0, gate0, hid0):
        self.name, self.pairs, self.kt = name, pairs, kt
        self.pair0, self.unit0, self.load0 = pair0, unit0, load0
        self.drained0, self.gate0, self.hid0 = drained0, gate0, hid0
        self.drains = 1 if name == "in" else 2
        self.used0 = unit0 - pair0
        self.upp = -(-kt // K_UNIT)
        self.units = pairs * self.upp
        self.loads = self.units // 2

    def k_of(self, v):
        a = v % self.upp * K_UNIT
        return range(a, min(a + K_UNIT, self.kt))


def plan():
    out, pair, unit, drained, gates, hids = [], 0, 0, 0, 0, 0
    for name, pairs, kt in PHASES:
        p = Phase(name, pairs, kt, pair, unit, unit // 2, drained, gates, hids)
        out.append(p)
        pair, unit, drained = pair + p.pairs, unit + p.units, drained + p.pairs * p.drains
        gates += pairs if name in ("in", "glu") else 0
        hids += pairs if name == "in" else 0
        assert p.units % SPLIT_SLOTS == 0 and p.pairs % PAIR_BANKS == 0
    return out


def unit_done(p, v):
    j, n = divmod(v, p.upp)
    if n == p.upp - 1:
        return True, p.pair0 + j + 1
    return False, p.used0 + j * (p.upp - 1) + n + 1


def free_at(phases, gp):
    p = [p for p in phases if p.pair0 <= gp][-1]
    return p.drained0 + (gp - p.pair0) * p.drains + (1 if p.name == "glu" else p.drains)


def trunk(nc, io, out):
    phases = plan()
    all_units = [(p, v) for p in phases for v in range(p.units)]

    ctx = ExitStack()

    def sb(name, shape, dt=F32, where=None):
        return (where or ctx).enter_context(nc.sbuf_tensor(name, shape, dt))

    def sem(name):
        return ctx.enter_context(nc.semaphore(name))

    with ctx:
        raw = sb("raw", [P, RAW_SLOTS, 2 * UW])
        w_hi = sb("w_hi", [P, SPLIT_SLOTS, UW], F32R)
        w_lo = sb("w_lo", [P, SPLIT_SLOTS, UW], F32R)
        x_hi = sb("x_hi", [P, DT, TOK], F32R)
        x_lo = sb("x_lo", [P, DT, TOK], F32R)
        h = sb("h", [P, DT, TOK])
        ident = sb("ident", [P, P])
        ones = sb("ones", [P, P])
        gate = sb("gate", [P, TOK])
        prod = sb("prod", [P, 2, TOK])
        xf = sb("xf", [P, 2, TOK])
        sq = sb("sq", [P, 2, TOK])
        gains = sb("gains", [P, NORMS, DT])
        skip = sb("skip", [P, DT])
        ms = sb("ms", [P, TT])
        mhalf = sb("mhalf", [P, TT])
        rs = sb("rs", [P, TT])
        half = sb("half", [P, 2])
        diag = sb("diag", [P, TT, P])
        with ExitStack() as area:
            w2_bd = sb("w2_bd", [P, 2, 2, STEP, PPT, 32], F32, area)
            c_bd = sb("c_bd", [P, 3, 2, PPT, STEP + 1, 32], F32, area)
            decay = sb("decay", [P, 2, PPT, CH], F32, area)
            um = sb("um", [P, PPT, TOK], F32, area)
            w2_t = sb("w2_t", [P, 2, 2, STEP, P], F32, area)
            k_t = sb("k_t", [P, 2, STEP, 32], F32, area)
            rot_a = sb("rot_a", [P, 2, PPT, CH], F32, area)
            rot_b = sb("rot_b", [P, 2, PPT, CH], F32, area)
        y, z = sq, prod
        hid_hi = sb("hid_hi", [P, FT, TOK], F32R)
        hid_lo = sb("hid_lo", [P, FT, TOK], F32R)
        with ExitStack() as area:
            w2 = sb("w2", [P, 2, STEP, GP, S5_J], F32, area)
            cp = sb("cp", [P, 2, GP, STEP + 1, S5_J], F32, area)
            rotc = sb("rotc", [P, GP, CH], F32, area)
            rots = sb("rots", [P, GP, CH], F32, area)
            sm = sb("sm", [P, SMALLS, GP], F32, area)
            with ExitStack() as inner:
                tmp = sb("tmp", [P, 4, GP * S5_J], F32, inner)
            rot_in = sb("rot_in", [P, 2, PPT, CH], F32, area)
            scan = sb("scan", [P, 2, PPT, CH], F32, area)
            states = sb("states", [P, 2, 2, PPT, CH], F32, area)
            u = sb("u", [P, 3, TOK], F32, area)
        k_sb = sb("k_sb", [P, DT, TOK])
        v_sb = sb("v_sb", [P, TT, D])
        q_sb = sb("q_sb", [P, DT, TOK])
        dist = sb("dist", [P, P + TOK])
        sc = sb("sc", [P, 2, P + TOK])
        pr = sb("pr", [P, 3, P + TOK])
        pt = sb("pt", [P, 2, TOK + P])
        mx = sb("mx", [P, HEADS, 2, TT])
        sums = sb("sums", [P, HEADS, 2, TT])

        ps = ctx.enter_context(nc.psum_tensor("ps", [P, 8, 512], F32))
        SS, RB, TA, TB = 4, 5, 6, 7

        landed = [sem(f"landed{i}") for i in range(RAW_SLOTS)]
        hi_done = sem("hi_done")
        lo_done = sem("lo_done")
        unit_used = sem("unit_used")
        pair_done = sem("pair_done")
        drained = sem("drained")
        gate_ready = sem("gate_ready")
        hid_hi_done = sem("hid_hi_done")
        hid_ready = sem("hid_ready")
        x_in = sem("x_in")
        par_in = sem("par_in")
        s5_in = sem("s5_in")
        consts = sem("consts")
        sq_ready = sem("sq_ready")
        ss_done = sem("ss_done")
        ms_ready = sem("ms_ready")
        rs_ready = sem("rs_ready")
        diag_ready = sem("diag_ready")
        rb_ready = sem("rb_ready")
        xf_ready = sem("xf_ready")
        x_hi_done = sem("x_hi_done")
        x_ready = sem("x_ready")
        s5_exp = sem("s5_exp")
        s5_small = sem("s5_small")
        pool_step = sem("pool_step")
        u_ready = sem("u_ready")
        um_zero = sem("um_zero")
        um_ready = sem("um_ready")
        bd_ready = sem("bd_ready")
        prep_done = sem("prep_done")
        prep_copied = sem("prep_copied")
        v_done = sem("v_done")
        dve_step = sem("dve_step")
        st_ready = sem("st_ready")
        y_done = sem("y_done")
        yf_ready = sem("yf_ready")
        z_ready = sem("z_ready")
        dist_ready = sem("dist_ready")
        s_done = sem("s_done")
        mx_ready = sem("mx_ready")
        exp_done = sem("exp_done")
        pr_ready = sem("pr_ready")
        t_done = sem("t_done")
        pt_ready = sem("pt_ready")
        o_done = sem("o_done")
        out_ready = sem("out_ready")
        out_sent = sem("out_sent")

        weights = [io[n] for n in ("in0", "out0", "glu", "in1", "out1", "k", "v", "in2", "out2",
                                   "q", "o", "in3", "out3")]

        made = {}
        block = ctx.enter_context(nc.Block())

        @block.sync
        def _(sp):
            sp.dma_start(h[:, :, :], io["x"]).then_inc(x_in, 16)

            def load(n, c, i=0):
                p = phases[n]
                g = p.load0 + c
                if g >= RAW_SLOTS:
                    sp.wait_ge(lo_done, 2 * (g - RAW_SLOTS + 1) + 8 * i)
                per = p.upp // 2
                a = c % per * 2 * UW
                w = min(2 * UW, p.kt * 2 * P - a)
                src = weights[n][c // per + (4 * i if per == 1 else 0), :, a:a + w]
                sp.dma_start(raw[:, g % RAW_SLOTS, 0:w], src).then_inc(landed[g % RAW_SLOTS], 16)

            for n, p in enumerate(phases):
                if p.name == "in":
                    for c in range(4):
                        load(n, c)
                    with sp.Fori(0, p.loads // 4 - 1) as i:
                        for c in range(4, 8):
                            load(n, c, i)
                    for c in range(p.loads // 4 * 4, p.loads):
                        load(n, c)
                else:
                    for c in range(p.loads):
                        load(n, c)
            for d in range(DT):
                sp.wait_ge(out_ready, d + 1)
                sp.dma_start(out[:, d, :], h[:, d, :]).then_inc(out_sent, 16)
            sp.wait_ge(out_sent, 16 * DT)

        @block.gpsimd
        def _(pool):
            pool.memset(ident[:, :], 0.0).then_inc(pool_step, 1)
            pool.memset(mhalf[:, :], -0.5).then_inc(consts, 1)
            pool.memset(ones[:, :], 1.0).then_inc(consts, 1)
            pool.wait_ge(pool_step, 1)
            pool.affine_select(out=ident[:, :], in_=ident[:, :], compare_op=ALU.not_equal, fill=1.0,
                               base=0, pattern=[[-1, P]], channel_multiplier=1).then_inc(consts, 1)
            pool.memset(half[:, :], 1.0).then_inc(pool_step, 1)
            pool.wait_ge(pool_step, 2)
            pool.affine_select(out=half[:, 0:1], in_=half[:, 0:1], compare_op=ALU.is_ge, fill=0.0,
                               base=S5_N - 1, pattern=[[0, 1]], channel_multiplier=-1)\
                .then_inc(pool_step, 1)
            pool.affine_select(out=half[:, 1:2], in_=half[:, 1:2], compare_op=ALU.is_ge, fill=0.0,
                               base=-S5_N, pattern=[[0, 1]], channel_multiplier=1)\
                .then_inc(pool_step, 1)
            norms = [0]

            def inverse_rms():
                norms[0] += 1
                pool.wait_ge(ms_ready, norms[0])
                pool.tensor_tensor(rs[:, :], ms[:, :], mhalf[:, :], ALU.pow).then_inc(rs_ready, 1)

            steps = [4]

            def link(ins):
                ins.then_inc(pool_step, 1)
                steps[0] += 1
                pool.wait_ge(pool_step, steps[0])

            def tt(o, a, b, op):
                link(pool.tensor_tensor(o, a, b, op))

            def ts(o, a, s1, s2, op0=ALU.mult, op1=ALU.add):
                link(pool.tensor_scalar(o, a, s1, s2, op0, op1))

            (A_RE, A_IM, LS, DTM, XA, TH, KK, RR, COS, MAG, SIN, HALF, LR, LI, NR, DEN, FR, FI,
             T1, T2, PR, PI, QR, QI, MAG4, UR, UI) = range(27)

            def s(i):
                return sm[:, i, :]

            def cmul(o_r, o_i, a_r, a_i, b_r, b_i, t1, t2):
                tt(t1, a_r, b_r, ALU.mult)
                tt(t2, a_i, b_i, ALU.mult)
                tt(o_r, t1, t2, ALU.subtract)
                tt(t1, a_r, b_i, ALU.mult)
                tt(t2, a_i, b_r, ALU.mult)
                tt(o_i, t1, t2, ALU.add)

            pool.wait_ge(s5_in, 16 * S5_LOADS)
            ts(s(A_RE), s(A_RE), -1e-4, 0.0, ALU.min, ALU.add)
            pool.wait_ge(s5_exp, 1)
            tt(s(XA), s(A_RE), s(DTM), ALU.mult)
            tt(s(TH), s(A_IM), s(DTM), ALU.mult)
            ts(s(KK), s(TH), 1.0 / (2.0 * math.pi), ROUND)
            ts(s(KK), s(KK), -ROUND, 0.0, ALU.add, ALU.add)
            ts(s(T1), s(KK), -TWO_PI[0], 0.0)
            tt(s(RR), s(TH), s(T1), ALU.add)
            ts(s(T1), s(KK), -TWO_PI[1], 0.0)
            tt(s(RR), s(RR), s(T1), ALU.add)
            ts(s(T1), s(KK), -TWO_PI[2], 0.0)
            tt(s(RR), s(RR), s(T1), ALU.add)
            pool.tensor_scalar(s(RR), s(RR), PI_LOW, -PI_LOW, ALU.min, ALU.max)\
                .then_inc(s5_small, 1)
            pool.wait_ge(s5_exp, 4)
            inverse_rms()
            tt(s(COS), s(HALF), s(HALF), ALU.mult)
            ts(s(COS), s(COS), -2.0, 1.0)
            tt(s(LR), s(MAG), s(COS), ALU.mult)
            tt(s(LI), s(MAG), s(SIN), ALU.mult)
            ts(s(NR), s(LR), 1.0, -1.0)
            tt(s(T1), s(A_RE), s(A_RE), ALU.mult)
            tt(s(T2), s(A_IM), s(A_IM), ALU.mult)
            tt(s(DEN), s(T1), s(T2), ALU.add)
            tt(s(T1), s(NR), s(A_RE), ALU.mult)
            tt(s(T2), s(LI), s(A_IM), ALU.mult)
            tt(s(T1), s(T1), s(T2), ALU.add)
            link(pool.memset(s(T2), -1.0))
            tt(s(DEN), s(DEN), s(T2), ALU.pow)
            tt(s(FR), s(T1), s(DEN), ALU.mult)
            tt(s(T1), s(LI), s(A_RE), ALU.mult)
            tt(s(T2), s(NR), s(A_IM), ALU.mult)
            tt(s(T1), s(T1), s(T2), ALU.subtract)
            tt(s(FI), s(T1), s(DEN), ALU.mult)

            def wide(i):
                return s(i).unsqueeze(2).broadcast_to([P, GP, S5_J])

            def t(i):
                return tmp[:, i, :].rearrange("p (g j) -> p g j", j=S5_J)

            cmul(w2[:, 0, STEP - 1], w2[:, 1, STEP - 1], t(0), t(1), wide(FR), wide(FI), t(2), t(3))
            for k in range(STEP - 2, -1, -1):
                cmul(w2[:, 0, k], w2[:, 1, k], w2[:, 0, k + 1], w2[:, 1, k + 1], wide(LR), wide(LI),
                     t(2), t(3))
            for k in range(1, STEP + 1):
                cmul(cp[:, 0, :, k], cp[:, 1, :, k], cp[:, 0, :, k - 1], cp[:, 1, :, k - 1],
                     wide(LR), wide(LI), t(2), t(3))
            ts(cp[:, 1], cp[:, 1], -1.0, 0.0)
            tt(s(T1), s(MAG), s(MAG), ALU.mult)
            tt(s(MAG4), s(T1), s(T1), ALU.mult)
            cmul(s(PR), s(PI), s(COS), s(SIN), s(COS), s(SIN), s(T1), s(T2))
            cmul(s(UR), s(UI), s(PR), s(PI), s(PR), s(PI), s(T1), s(T2))
            link(pool.memset(rotc[:, :, 0:1], 1.0))
            link(pool.memset(rots[:, :, 0:1], 0.0))
            w, cur, nxt = 1, (UR, UI), (QR, QI)
            while w < CH:
                def b(i):
                    return s(i).unsqueeze(2).broadcast_to([P, GP, w])

                def part(k):
                    a = tmp[:, 2 * k:2 * k + 2, :].rearrange("p a x -> p (a x)")[:, 0:GP * w]
                    return a.rearrange("p (g c) -> p g c", c=w)

                cmul(rotc[:, :, w:2 * w], rots[:, :, w:2 * w], rotc[:, :, 0:w], rots[:, :, 0:w],
                     b(cur[0]), b(cur[1]), part(0), part(1))
                cmul(s(nxt[0]), s(nxt[1]), s(cur[0]), s(cur[1]), s(cur[0]), s(cur[1]), s(T1), s(T2))
                w, cur, nxt = 2 * w, nxt, cur
            made["s5"] = steps[0]
            inverse_rms()

            pool.memset(um[:, :, :], 0.0).then_inc(um_zero, 1)
            for d in range(DT):
                b = d % 2
                if d >= 2:
                    pool.wait_ge(prep_done, d - 1)
                for g in range(2):
                    cols = slice(S5_J * g, S5_J * g + S5_J)
                    for r in range(2):
                        pool.tensor_scalar(w2_bd[:, b, r, :, :, cols],
                                           w2[:, r, :, PPT * d:PPT * d + PPT, :],
                                           half[:, g:g + 1], 0.0,
                                           ALU.mult, ALU.add).then_inc(bd_ready, 1)
                if d >= 3:
                    pool.wait_ge(y_done, d - 2)
                for g in range(2):
                    cols = slice(S5_J * g, S5_J * g + S5_J)
                    for r in range(2):
                        pool.tensor_scalar(c_bd[:, d % 3, r, :, :, cols],
                                           cp[:, r, PPT * d:PPT * d + PPT, :, :],
                                           half[:, g:g + 1], 0.0,
                                           ALU.mult, ALU.add).then_inc(bd_ready, 1)
                if d >= 2:
                    pool.wait_ge(st_ready, 2 * (d - 1))
                pool.tensor_scalar(decay[:, b, :, 1:CH],
                                   s(MAG4)[:, PPT * d:PPT * d + PPT].unsqueeze(2)
                                   .broadcast_to([P, PPT, CH - 1]),
                                   1.0, 0.0, ALU.mult, ALU.add).then_inc(bd_ready, 1)
                pool.memset(decay[:, b, :, 0:1], 0.0).then_inc(bd_ready, 1)
            for _ in range(2):
                inverse_rms()
            for q0, c0, w in ((0, 0, P), (P, P, TOK)):
                part = dist[:, c0:c0 + w]
                pool.iota(part, [[1, w]], base=-q0, channel_multiplier=-1,
                          allow_small_or_imprecise_dtypes=True).then_inc(dist_ready, 1)
            pool.wait_ge(dist_ready, 2)
            for q0, c0, w in ((0, 0, P), (P, P, TOK)):
                part = dist[:, c0:c0 + w]
                pool.affine_select(out=part, in_=part, compare_op=ALU.is_ge, fill=NEG, base=q0,
                                   pattern=[[-1, w]], channel_multiplier=1).then_inc(dist_ready, 1)
            for _ in range(3):
                inverse_rms()

        @block.scalar
        def _(act):
            act.dma_start(gains[:, :, :], io["gains"]).then_inc(par_in, 16)
            act.dma_start(skip[:, :], io["skip"]).then_inc(par_in, 16)
            act.dma_start(sm[:, 0, :], io["a_re"]).then_inc(s5_in, 16)
            act.dma_start(sm[:, 1, :], io["a_im"]).then_inc(s5_in, 16)
            for g in range(2):
                act.dma_start(sm[64 * g:64 * g + 64, 2, :],
                              io["log_step"][g:g + 1, :].broadcast_to([64, GP])).then_inc(s5_in, 16)
            act.dma_start(tmp[:, 0, :], io["b_re"]).then_inc(s5_in, 16)
            act.dma_start(tmp[:, 1, :], io["b_im"]).then_inc(s5_in, 16)
            act.dma_start(cp[:, 0, :, 0, :], io["c_re"].rearrange("p (g j) -> p g j", j=S5_J)).then_inc(s5_in, 16)
            act.dma_start(cp[:, 1, :, 0, :], io["c_im"].rearrange("p (g j) -> p g j", j=S5_J)).then_inc(s5_in, 16)

            def split(gu, i=0):
                if gu >= len(all_units):
                    return
                p, v = all_units[gu]
                ld = gu // 2
                w = len(p.k_of(v)) * 2 * P
                if gu % 2 == 0:
                    act.wait_ge(landed[ld % RAW_SLOTS], 16 * (ld // RAW_SLOTS + 1) + 16 * i)
                if gu >= SPLIT_SLOTS:
                    last, value = unit_done(*all_units[gu - SPLIT_SLOTS])
                    act.wait_ge(pair_done if last else unit_used, value + 4 * i)
                a = gu % 2 * UW
                act.activation(w_hi[:, gu % SPLIT_SLOTS, 0:w], raw[:, ld % RAW_SLOTS, a:a + w],
                               ACT.Copy).then_inc(hi_done, 1)

            def square(d, ready, count):
                act.wait_ge(drained, ready)
                if count >= 2:
                    act.wait_ge(ss_done, count - 1)
                act.activation(sq[:, count % 2, :], h[:, d, :], ACT.Square).then_inc(sq_ready, 1)

            def high_x(count, d):
                act.wait_ge(xf_ready, count + 1)
                act.activation(x_hi[:, d, :], xf[:, count % 2, :], ACT.Copy).then_inc(x_hi_done, 1)

            tally = {"sq": 0, "xf": 0}

            def squares(tiles, ready):
                for n, d in enumerate(tiles):
                    square(d, ready + n, tally["sq"])
                    tally["sq"] += 1

            def norm_x():
                for d in range(DT):
                    high_x(tally["xf"], d)
                    tally["xf"] += 1

            def drain(p, j, i=0):
                gp = p.pair0 + j
                if p.name == "in":
                    act.wait_ge(pair_done, gp + 1 + 4 * i)
                    act.activation(gate[:, :], ps[:, 2 * (gp % 2), 0:TOK], ACT.Silu)\
                       .then_inc(gate_ready, 1)
                    act.wait_ge(drained, p.drained0 + j + 1 + 4 * i)
                    act.activation(hid_hi[:, j + 4 * i, :], prod[:, gp % 2, :], ACT.Copy)\
                       .then_inc(hid_hi_done, 1)
                elif p.name == "glu":
                    act.wait_ge(pair_done, gp + 1)
                    act.activation(gate[:, :], ps[:, 2 * (gp % 2) + 1, 0:TOK], ACT.Sigmoid)\
                       .then_inc(gate_ready, 1)
                    squares([j], p.drained0 + 2 * j + 2)
                elif p.name in ("out", "o"):
                    squares([2 * j, 2 * j + 1], p.drained0 + 2 * j + 1)

            def phase(n):
                p = phases[n]

                def step(v, i=0):
                    split(p.unit0 + v + LEAD, i)
                    if v % p.upp == p.upp - 1:
                        drain(p, v // p.upp, i)

                if p.name == "in":
                    for v in range(8):
                        step(v)
                    with act.Fori(0, p.units // 8 - 1) as i:
                        for v in range(8, 16):
                            step(v, i)
                    for v in range(p.units // 8 * 8, p.units):
                        step(v)
                else:
                    for v in range(p.units):
                        step(v)

            for d in range(DT):
                if d == 0:
                    act.wait_ge(x_in, 16)
                if d >= 2:
                    act.wait_ge(ss_done, d - 1)
                act.activation(sq[:, d % 2, :], h[:, d, :], ACT.Square).then_inc(sq_ready, 1)
            tally["sq"] = DT
            act.wait_ge(s5_in, 16 * S5_LOADS)
            act.activation(sm[:, 3, :], sm[:, 2, :], ACT.Exp).then_inc(s5_exp, 1)
            act.wait_ge(s5_small, 1)
            act.activation(sm[:, 9, :], sm[:, 4, :], ACT.Exp).then_inc(s5_exp, 1)
            act.activation(sm[:, 10, :], sm[:, 7, :], ACT.Sin).then_inc(s5_exp, 1)
            act.activation(sm[:, 11, :], sm[:, 7, :], ACT.Sin, scale=0.5).then_inc(s5_exp, 1)
            split(0)
            split(1)
            norm_x()
            phase(0)
            phase(1)

            def prep_copy(d):
                act.wait_ge(prep_done, d + 1)
                if d >= 2:
                    act.wait_ge(v_done, d - 1)
                for r, bank in ((0, TA), (1, TB)):
                    act.activation(w2_t[:, d % 2, r, :, :].rearrange("p s x -> p (s x)"), ps[:, bank, :],
                                   ACT.Copy).then_inc(prep_copied, 1)
                if d >= 2:
                    act.wait_ge(y_done, d - 1)
                act.activation(k_t[:, d % 2, :, :].rearrange("p s x -> p (s x)"),
                               ps[:, SS, 0:P], ACT.Copy).then_inc(prep_copied, 1)

            def gelu(d):
                act.wait_ge(yf_ready, d + 1)
                if d >= 2:
                    act.wait_ge(x_ready, DT + d - 1)
                act.activation(z[:, d % 2, :], y[:, d % 2, :], ACT.Gelu_apprx_tanh)\
                   .then_inc(z_ready, 1)
                act.wait_ge(z_ready, d + 1)
                act.activation(x_hi[:, d, :], z[:, d % 2, :], ACT.Copy).then_inc(x_hi_done, 1)

            def part_pairs(d):
                act.wait_ge(u_ready, d + 1)
                if d == 0:
                    act.wait_ge(um_zero, 1)
                if d >= 1:
                    act.wait_ge(v_done, d)
                for g in range(PPT):
                    rows = slice(32 * g, 32 * g + 32)
                    act.activation(um[rows, g, :], u[rows, d % 3, :], ACT.Copy)\
                       .then_inc(um_ready, 1)

            part_pairs(0)
            prep_copy(0)
            prep_copy(1)
            for d in range(DT):
                if d + 1 < DT:
                    part_pairs(d + 1)
                if d + 2 < DT:
                    prep_copy(d + 2)
                if d >= 1:
                    gelu(d - 1)
            gelu(DT - 1)
            phase(2)
            norm_x()
            phase(3)
            phase(4)
            norm_x()
            phase(5)
            phase(6)
            norm_x()
            phase(7)
            phase(8)
            norm_x()
            phase(9)

            def exps(n):
                act.wait_ge(mx_ready, n + 1)
                if n >= 3:
                    act.wait_ge(t_done, n - 2)
                for q, a, w in ((0, 0, P), (1, P, TOK)):
                    act.activation(pr[:, n % 3, a:a + w], sc[:, n % 2, a:a + w], ACT.Exp,
                                   bias=mx[:, n, 1, q:q + 1],
                                   accum_out=sums[:, n, 0, q:q + 1]).then_inc(exp_done, 1)

            def pt_copy(n):
                act.wait_ge(t_done, n + 1)
                if n >= 2:
                    act.wait_ge(o_done, n - 1)
                act.activation(pt[:, n % 2, :], ps[:, 2 + n % 2, 0:TOK + P], ACT.Copy)\
                   .then_inc(pt_ready, 1)

            def high_o(n):
                act.wait_ge(o_done, n + 1)
                act.activation(x_hi[:, n // 2, :], ps[:, 6 + n // 2 % 2, 0:TOK], ACT.Copy)\
                   .then_inc(x_hi_done, 1)

            for n in range(HEADS + 4):
                if n < HEADS:
                    exps(n)
                if 2 <= n < HEADS + 2:
                    pt_copy(n - 2)
                if n >= 4 and (n - 4) % 2 == 1:
                    high_o(n - 4)
            phase(10)
            norm_x()
            phase(11)
            phase(12)

        @block.vector
        def _(dve):
            tally = {"xf": 0, "x": 0, "norm": 0, "step": 0}

            def link(ins):
                ins.then_inc(dve_step, 1)
                tally["step"] += 1
                dve.wait_ge(dve_step, tally["step"])

            def split(gu, i=0):
                if gu >= len(all_units):
                    return
                p, v = all_units[gu]
                w = len(p.k_of(v)) * 2 * P
                a = gu % 2 * UW
                dve.wait_ge(hi_done, gu + 1 + 8 * i)
                dve.tensor_tensor(w_lo[:, gu % SPLIT_SLOTS, 0:w],
                                  raw[:, gu // 2 % RAW_SLOTS, a:a + w],
                                  w_hi[:, gu % SPLIT_SLOTS, 0:w].bitcast(F32),
                                  ALU.subtract).then_inc(lo_done, 1)

            def low_x(src):
                dve.wait_ge(x_hi_done, tally["x"] + 1)
                d = tally["x"] % DT
                dve.tensor_tensor(x_lo[:, d, :], src, x_hi[:, d, :].bitcast(F32), ALU.subtract)\
                   .then_inc(x_ready, 1)
                tally["x"] += 1

            def rms():
                tally["norm"] += 1
                n = tally["norm"]
                dve.wait_ge(ss_done, DT * n)
                dve.tensor_scalar(ms[:, :], ps[:, SS, 0:TT], 1.0 / D, EPS, ALU.mult, ALU.add)\
                   .then_inc(ms_ready, 1)
                dve.wait_ge(rs_ready, n)
                dve.wait_ge(consts, 3)
                for q in range(TT):
                    dve.tensor_scalar(diag[:, q, :], ident[:, :], rs[:, q:q + 1], None, ALU.mult)\
                       .then_inc(diag_ready, 1)
                dve.wait_ge(rb_ready, n)

            def normed(dst, d, g):
                return dve.scalar_tensor_tensor(dst, h[:, d, :], gains[:, g, d:d + 1],
                                                ps[:, RB, 0:TOK], ALU.mult, ALU.mult)

            def norm_x(g):
                for d in range(DT + 1):
                    if d < DT:
                        k = tally["xf"]
                        if k >= 2:
                            dve.wait_ge(x_ready, tally["x"])
                        normed(xf[:, k % 2, :], d, g).then_inc(xf_ready, 1)
                        tally["xf"] += 1
                    if d >= 1:
                        low_x(xf[:, (tally["xf"] - (2 if d < DT else 1)) % 2, :])

            def drain(p, j, i=0):
                gp = p.pair0 + j
                b = 2 * (gp % 2)
                if p.name == "in":
                    dve.wait_ge(gate_ready, p.gate0 + j + 1 + 4 * i)
                    dve.tensor_tensor(prod[:, gp % 2, :], gate[:, :], ps[:, b + 1, 0:TOK], ALU.mult)\
                       .then_inc(drained, 1)
                    dve.wait_ge(hid_hi_done, p.hid0 + j + 1 + 4 * i)
                    dve.tensor_tensor(hid_lo[:, j + 4 * i, :], prod[:, gp % 2, :],
                                      hid_hi[:, j + 4 * i, :].bitcast(F32), ALU.subtract)\
                       .then_inc(hid_ready, 1)
                    return
                if p.name == "glu":
                    dve.wait_ge(gate_ready, p.gate0 + j + 1)
                    dve.tensor_tensor(prod[:, gp % 2, :], gate[:, :], ps[:, b, 0:TOK], ALU.mult)\
                       .then_inc(drained, 1)
                    dve.wait_ge(drained, p.drained0 + 2 * j + 1)
                    dve.tensor_tensor(h[:, j, :], h[:, j, :], prod[:, gp % 2, :], ALU.add)\
                       .then_inc(drained, 1)
                    return
                dve.wait_ge(pair_done, gp + 1)
                for m in range(2):
                    src = ps[:, b + m, 0:TOK]
                    d = 2 * j + m
                    if p.name in ("out", "o"):
                        ins = dve.scalar_tensor_tensor(h[:, d, :], src,
                                                       0.5 if p.name == "out" else 1.0,
                                                       h[:, d, :], ALU.mult, ALU.add)
                    elif p.name == "k":
                        ins = dve.tensor_copy(k_sb[:, d, :], src)
                    elif p.name == "v":
                        ins = dve.tensor_copy(v_sb[:, m, 2 * P * j:2 * P * j + 2 * P], src)
                    else:
                        ins = dve.tensor_scalar(q_sb[:, d, :], src, HD ** -0.5, None, ALU.mult)
                    ins.then_inc(drained, 1)

            def phase(n):
                p = phases[n]

                def step(v, i=0):
                    split(p.unit0 + v + LEAD, i)
                    if v % p.upp == p.upp - 1:
                        drain(p, v // p.upp, i)

                if p.name == "in":
                    with dve.Fori(0, p.units // 8) as i:
                        for v in range(8):
                            step(v, i)
                    for v in range(p.units // 8 * 8, p.units):
                        step(v)
                else:
                    for v in range(p.units):
                        step(v)

            rms()
            split(0)
            split(1)
            dve.wait_ge(par_in, 32)
            norm_x(0)
            phase(0)
            phase(1)

            rms()
            dve.wait_ge(pool_step, made["s5"])

            def mixer_input(d):
                if d >= 3:
                    dve.wait_ge(um_ready, PPT * (d - 2))
                    dve.wait_ge(yf_ready, d - 2)
                normed(u[:, d % 3, :], d, 1).then_inc(u_ready, 1)

            def turn(dst_r, dst_i, src_r, src_i, d, back):
                g = slice(PPT * d, PPT * d + PPT)
                cs, sn = rotc[:, g, :], rots[:, g, :]
                dve.tensor_tensor(rot_a[:, 0], src_r, cs, ALU.mult).then_inc(dve_step, 1)
                dve.tensor_tensor(rot_b[:, 0], src_i, sn, ALU.mult).then_inc(dve_step, 1)
                dve.tensor_tensor(rot_a[:, 1], src_i, cs, ALU.mult).then_inc(dve_step, 1)
                dve.tensor_tensor(rot_b[:, 1], src_r, sn, ALU.mult).then_inc(dve_step, 1)
                tally["step"] += 4
                dve.wait_ge(dve_step, tally["step"])
                plus, minus = (ALU.subtract, ALU.add) if back else (ALU.add, ALU.subtract)
                return (dve.tensor_tensor(dst_r, rot_a[:, 0], rot_b[:, 0], plus),
                        dve.tensor_tensor(dst_i, rot_a[:, 1], rot_b[:, 1], minus))

            def scan_tile(d):
                b = d % 2
                v = ps[:, b, :].rearrange("p (r g c) -> p r g c", r=2, c=CH)
                dve.wait_ge(v_done, d + 1)
                for ins in turn(rot_in[:, 0], rot_in[:, 1], v[:, 0], v[:, 1], d, False):
                    ins.then_inc(dve_step, 1)
                tally["step"] += 2
                dve.wait_ge(dve_step, tally["step"])
                dve.wait_ge(bd_ready, BD_STEPS * (d + 1))
                for r in range(2):
                    dve.tensor_tensor_scan(scan[:, r].rearrange("p g c -> p (g c)"),
                                           decay[:, b].rearrange("p g c -> p (g c)"),
                                           rot_in[:, r].rearrange("p g c -> p (g c)"),
                                           0.0, ALU.mult, ALU.add).then_inc(dve_step, 1)
                tally["step"] += 2
                dve.wait_ge(dve_step, tally["step"])
                if d >= 2:
                    dve.wait_ge(y_done, d - 1)
                for ins in turn(states[:, b, 0], states[:, b, 1], scan[:, 0], scan[:, 1], d, True):
                    ins.then_inc(st_ready, 1)

            def add_skip(d):
                dve.wait_ge(y_done, d + 1)
                if d >= 2:
                    dve.wait_ge(z_ready, d - 1)
                dve.scalar_tensor_tensor(y[:, d % 2, :], u[:, d % 3, :], skip[:, d:d + 1],
                                         ps[:, 2 + d % 2, 0:TOK], ALU.mult, ALU.add)\
                   .then_inc(yf_ready, 1)

            mixer_input(0)
            for d in range(DT + 2):
                if d + 1 < DT:
                    mixer_input(d + 1)
                if d < DT:
                    if d >= 1:
                        dve.wait_ge(st_ready, 2 * d)
                    scan_tile(d)
                if 1 <= d <= DT:
                    add_skip(d - 1)
                if d >= 2:
                    low_x(z[:, d % 2, :])
            phase(2)
            rms()
            norm_x(2)
            phase(3)
            phase(4)
            rms()
            norm_x(3)
            phase(5)
            phase(6)
            norm_x(4)
            phase(7)
            phase(8)
            rms()
            norm_x(5)
            phase(9)

            dve.wait_ge(dist_ready, 4)

            def shifted_max(n):
                b = n % 2
                dve.wait_ge(s_done, n + 1)
                if n >= 2:
                    dve.wait_ge(exp_done, 2 * (n - 1))
                slope = 2.0 ** (-8.0 * (n + 1) / HEADS)
                link(dve.scalar_tensor_tensor(sc[:, b, :], dist[:, :], slope,
                                              ps[:, b, 0:P + TOK], ALU.mult, ALU.add))
                for q, a, w in ((0, 0, P), (1, P, TOK)):
                    ins = dve.reduce_max(mx[:, n, 0, q:q + 1], sc[:, b, a:a + w], AX_X)
                    ins.then_inc(dve_step, 1)
                tally["step"] += 2
                dve.wait_ge(dve_step, tally["step"])
                dve.tensor_scalar(mx[:, n, 1, :], mx[:, n, 0, :], -1.0, None, ALU.mult)\
                   .then_inc(mx_ready, 1)

            def normalise(n):
                dve.wait_ge(exp_done, 2 * (n + 1))
                link(dve.reciprocal(sums[:, n, 1, :], sums[:, n, 0, :]))
                for q, a, w in ((0, 0, P), (1, P, TOK)):
                    dve.tensor_scalar(pr[:, n % 3, a:a + w], pr[:, n % 3, a:a + w],
                                      sums[:, n, 1, q:q + 1], None, ALU.mult).then_inc(pr_ready, 1)

            for n in range(HEADS + 4):
                if n < HEADS:
                    shifted_max(n)
                if 1 <= n <= HEADS:
                    normalise(n - 1)
                if n >= 4 and (n - 4) % 2 == 1:
                    low_x(ps[:, 6 + (n - 4) // 2 % 2, 0:TOK])
            phase(10)
            rms()
            norm_x(6)
            phase(11)
            phase(12)
            rms()
            for d in range(DT):
                normed(h[:, d, :], d, 7).then_inc(out_ready, 1)

        @block.tensor
        def _(pe):
            tally = {"sq": 0, "norm": 0, "x": 0}

            def mm(o, w, x, start, stop, **kw):
                return pe.matmul(o, w, x, start=start, stop=stop, skip_group_check=True, **kw)

            def sum_squares(tiles):
                for d in tiles:
                    k = tally["sq"]
                    pe.wait_ge(sq_ready, k + 1)
                    if k == 0:
                        pe.wait_ge(consts, 3)
                    for q in range(TT):
                        last = mm(ps[:, SS, q:q + 1], sq[:, k % 2, q * P:q * P + P], ones[:, 0:1],
                                  d == 0 and q == 0, d == DT - 1)
                    last.then_inc(ss_done, 1)
                    tally["sq"] += 1

            def broadcast():
                tally["norm"] += 1
                pe.wait_ge(diag_ready, TT * tally["norm"])
                for q in range(TT):
                    last = mm(ps[:, RB, q * P:q * P + P], ones[:, :], diag[:, q, :], True, True)
                last.then_inc(rb_ready, 1)

            def pair(p, j, i=0, first=False):
                gp = p.pair0 + j
                if gp >= PAIR_BANKS:
                    pe.wait_ge(drained, free_at(phases, gp - PAIR_BANKS) + p.drains * 2 * i)
                b = 2 * (gp % 2)
                hi, lo = (hid_hi, hid_lo) if p.name == "out" else (x_hi, x_lo)
                for n in range(p.upp):
                    gu = p.unit0 + j * p.upp + n
                    s = gu % SPLIT_SLOTS
                    pe.wait_ge(lo_done, gu + 1 + 2 * p.upp * i)
                    for k in p.k_of(n):
                        if first:
                            if p.name == "out":
                                pe.wait_ge(hid_ready, p.hid0 - FT + k + 1)
                            else:
                                pe.wait_ge(x_ready, tally["x"] + k + 1)
                        st, sp_ = k == 0, k == p.kt - 1
                        a = (k - n * K_UNIT) * 2 * P
                        for m in range(2):
                            o = ps[:, b + m, 0:TOK]
                            if p.name == "v":
                                tok = slice(m * P, m * P + P)
                                mm(o, hi[:, k, tok], w_hi[:, s, a:a + 2 * P], st, False)
                                mm(o, hi[:, k, tok], w_lo[:, s, a:a + 2 * P], False, False)
                                last = mm(o, lo[:, k, tok], w_hi[:, s, a:a + 2 * P], False, sp_)
                            else:
                                w = slice(a + m * P, a + m * P + P)
                                mm(o, w_hi[:, s, w], hi[:, k, :], st, False)
                                mm(o, w_hi[:, s, w], lo[:, k, :], False, False)
                                last = mm(o, w_lo[:, s, w], hi[:, k, :], False, sp_)
                    if n < p.upp - 1:
                        last.then_inc(unit_used, 1)
                last.then_inc(pair_done, 1)

            def phase(n):
                p = phases[n]
                if p.name == "in":
                    pair(p, 0, first=True)
                    pair(p, 1)
                    with pe.Fori(0, p.pairs // 2 - 1) as i:
                        pair(p, 2, i)
                        pair(p, 3, i)
                else:
                    for j in range(p.pairs):
                        pair(p, j, first=j == 0 and p.name != "v")
                        if p.name in ("out", "o") and j >= 1:
                            sum_squares([2 * j - 2, 2 * j - 1])
                        if p.name == "glu" and j >= 1:
                            sum_squares([j - 1])
                    if p.name in ("out", "o"):
                        sum_squares([DT - 2, DT - 1])
                    if p.name == "glu":
                        sum_squares([DT - 1])
                if p.name not in ("out", "k"):
                    tally["x"] += DT

            sum_squares(range(DT))
            broadcast()
            phase(0)
            phase(1)
            broadcast()

            def prepare(d):
                b = d % 2
                pe.wait_ge(bd_ready, BD_STEPS * (d + 1))
                if d >= 1:
                    pe.wait_ge(prep_copied, 3 * d)
                for r, bank in ((0, TA), (1, TB)):
                    for t in range(STEP):
                        pe.transpose(ps[:, bank, t * P:t * P + P],
                                     w2_bd[:, b, r, t, :, :].rearrange("p g j -> p (g j)"),
                                     ident[:, :])
                for g in range(PPT):
                    rows = slice(32 * g, 32 * g + 32)
                    for r in range(2):
                        last = mm(ps[rows, SS, 0:P], w2_bd[:, b, r, STEP - 1, g, :],
                                  c_bd[:, d % 3, r, g, 0:STEP, :].rearrange("p t j -> p (t j)"),
                                  r == 0, r == 1)
                last.then_inc(prep_done, 1)

            def chunk_inputs(d):
                pe.wait_ge(prep_copied, 3 * (d + 1))
                pe.wait_ge(um_ready, PPT * (d + 1))
                if d >= 2:
                    pe.wait_ge(st_ready, 2 * (d - 1))
                us = um[:, :, :].rearrange("p g (c s) -> p s g c", s=STEP)
                for r in range(2):
                    a = r * PPT * CH
                    o = ps[:, d % 2, a:a + PPT * CH].rearrange("p (g c) -> p g c", c=CH)
                    for t in range(STEP):
                        last = mm(o, w2_t[:, d % 2, r, t, :], us[:, t, :, :], t == 0, t == STEP - 1)
                last.then_inc(v_done, 1)

            def outputs(d):
                b = d % 2
                if d >= 2:
                    pe.wait_ge(yf_ready, d - 1)
                uc = u[:, d % 3, :].rearrange("p (c s) -> p c s", s=STEP)
                yc = ps[:, 2 + b, 0:TOK].rearrange("p (c s) -> p c s", s=STEP)
                for g in range(PPT):
                    rows = slice(32 * g, 32 * g + 32)
                    for t in range(STEP):
                        mm(yc[rows, :, t:STEP], k_t[rows, b, t, :], uc[rows, :, 0:STEP - t],
                           t == 0, False)
                pe.wait_ge(st_ready, 2 * (d + 1))
                for g in range(PPT):
                    rows = slice(32 * g, 32 * g + 32)
                    for t in range(STEP):
                        for r in range(2):
                            last = mm(yc[rows, 1:CH, t], c_bd[:, d % 3, r, g, t + 1, :],
                                      states[:, b, r, g, 0:CH - 1], False, r == 1)
                last.then_inc(y_done, 1)

            prepare(0)
            chunk_inputs(0)
            prepare(1)
            for d in range(DT):
                if d + 1 < DT:
                    chunk_inputs(d + 1)
                outputs(d)
                if d + 2 < DT:
                    prepare(d + 2)
            phase(2)
            broadcast()
            phase(3)
            phase(4)
            broadcast()
            phase(5)
            phase(6)
            phase(7)
            phase(8)
            broadcast()
            phase(9)

            def scores(n):
                b, d = n % 2, n // 2
                rows = slice(HD * (n % 2), HD * (n % 2) + HD)
                if n == 0:
                    pe.wait_ge(drained, phases[10].drained0)
                if n >= 2:
                    pe.wait_ge(mx_ready, n - 1)
                for q, a, w in ((0, 0, P), (1, P, TOK)):
                    last = mm(ps[:, b, a:a + w], q_sb[rows, d, q * P:q * P + P], k_sb[rows, d, 0:w],
                              True, True)
                last.then_inc(s_done, 1)

            def turn_probs(n):
                pe.wait_ge(pr_ready, 2 * (n + 1))
                if n >= 2:
                    pe.wait_ge(pt_ready, n - 1)
                for a in range(3):
                    last = pe.transpose(ps[:, 2 + n % 2, a * P:a * P + P],
                                        pr[:, n % 3, a * P:a * P + P], ident[:, :])
                last.then_inc(t_done, 1)

            def head_output(n):
                bank = 6 + n // 2 % 2
                rows = slice(HD * (n % 2), HD * (n % 2) + HD)
                cols = slice(HD * n, HD * n + HD)
                pe.wait_ge(pt_ready, n + 1)
                if n >= 4:
                    pe.wait_ge(x_ready, tally["x"] + n // 2 - 1)
                mm(ps[rows, bank, 0:TOK], v_sb[:, 0, cols], pt[:, n % 2, 0:TOK], True, False)
                mm(ps[rows, bank, P:TOK], v_sb[:, 1, cols], pt[:, n % 2, TOK:TOK + P], False, True)\
                    .then_inc(o_done, 1)

            for n in range(HEADS + 3):
                if n < HEADS:
                    scores(n)
                if 2 <= n < HEADS + 2:
                    turn_probs(n - 2)
                if n >= 3:
                    head_output(n - 3)
            phase(10)
            broadcast()
            phase(11)
            phase(12)
            broadcast()


def kernel(**inputs):
    import numpy as _np
    import concourse.bacc as _bacc
    from concourse import mybir as _mybir
    from concourse.bass_utils import run_bass_kernel_spmd as _run

    x = {k: _np.asarray(v) for k, v in inputs.items()}

    def pairs(w, halves):
        r, c = w.shape
        if halves:
            w = w.reshape(r // P, P, 2, c // (2 * P), P).transpose(3, 1, 0, 2, 4)
        else:
            w = w.reshape(r // P, P, c // (2 * P), 2, P).transpose(2, 1, 0, 3, 4)
        return _np.ascontiguousarray(w.reshape(w.shape[0], P, -1))

    def tiles(v):
        return _np.ascontiguousarray(_np.moveaxis(v.reshape(v.shape[:-1] + (DT, P)), -1, 0))

    def states(v):
        v = v.reshape((GP, 2 * S5_N) + v.shape[2:])
        return _np.ascontiguousarray(_np.moveaxis(v, 1, 0).reshape(P, -1))

    arrays = {
        "x": _np.ascontiguousarray(x["x"][0].T.reshape(DT, P, TOK).transpose(1, 0, 2)),
        "gains": tiles(_np.stack([x["ffn1_norm"][0], x["mix_norm"][0], x["ffn2_norm"][0],
                                  x["kv_norm"], x["ffn1_norm"][1], x["mix_norm"][1],
                                  x["ffn2_norm"][1], x["final_norm"]])),
        "skip": tiles(x["s5_d"][0]),
        "a_re": states(x["s5_a_re"][0]), "a_im": states(x["s5_a_im"][0]),
        "log_step": _np.ascontiguousarray(x["s5_log_step"][0].reshape(GP, 2).T),
        "b_re": states(x["s5_b_re"][0]), "b_im": states(x["s5_b_im"][0]),
        "c_re": states(x["s5_c_re"][0].transpose(0, 2, 1)),
        "c_im": states(x["s5_c_im"][0].transpose(0, 2, 1)),
        "glu": pairs(x["s5_w_glu"][0], True),
        "k": pairs(x["w_kv"][:, :D], False), "v": pairs(x["w_kv"][:, D:], False),
        "q": pairs(x["w_q"][0], False), "o": pairs(x["w_o"][0], False),
    }
    for n, (layer, ffn) in enumerate(((0, 1), (0, 2), (1, 1), (1, 2))):
        arrays[f"in{n}"] = pairs(x[f"ffn{ffn}_w_in"][layer], True)
        arrays[f"out{n}"] = pairs(x[f"ffn{ffn}_w_out"][layer], False)

    nc = _bacc.Bacc("TRN2", target_bir_lowering=False, num_devices=1)
    io = {k: nc.dram_tensor(f"in_{k}", a.shape, _mybir.dt.from_np(a.dtype), kind="ExternalInput").ap()
          for k, a in arrays.items()}
    out = nc.dram_tensor("out_x", (P, DT, TOK), F32, kind="ExternalOutput").ap()
    trunk(nc, io, out)
    r = _run(nc, [{f"in_{k}": a for k, a in arrays.items()}], core_ids=[0])
    got = r.results[0]["out_x"]
    return _np.ascontiguousarray(got.transpose(2, 1, 0).reshape(1, TOK, D))
```

```python
import math
from contextlib import ExitStack

import concourse.bass as bass
from concourse import mybir

ALU = mybir.AluOpType
ACT = mybir.ActivationFunctionType
F32 = mybir.dt.float32
F32R = mybir.dt.float32r
AX_X = mybir.AxisListType.X

P = 128
TOK = 256
TT = TOK // P
D = 1024
DT = D // P
FF = 2816
FT = FF // P
HEADS = 16
HD = D // HEADS
EPS = 1e-6

S5_G, S5_J, S5_N = 64, 16, 64
GP = S5_G // 2
PPT = GP // DT
STEP = 4
CH = TOK // STEP

K_UNIT = 4
UW = K_UNIT * 2 * P
RAW_SLOTS = 4
SPLIT_SLOTS = 4
LEAD = 2
PAIR_BANKS = 2

NORMS = 8
SMALLS = 27
S5_LOADS = 8
BD_STEPS = 10
NEG = -1e30
ROUND = 1.5 * 2.0 ** 23
TWO_PI = (6.28125, 0.0019350051879882812, 2.0 * math.pi - 6.28125 - 0.0019350051879882812)
PI_LOW = 3.1415925

PHASES = [
    ("in", FT, DT), ("out", DT // 2, FT), ("glu", DT, DT), ("in", FT, DT), ("out", DT // 2, FT),
    ("k", DT // 2, DT), ("v", DT // 2, DT), ("in", FT, DT), ("out", DT // 2, FT),
    ("q", DT // 2, DT), ("o", DT // 2, DT), ("in", FT, DT), ("out", DT // 2, FT),
]


class Phase:

    def __init__(self, name, pairs, kt, pair0, unit0, load0, drained0, gate0, hid0):
        self.name, self.pairs, self.kt = name, pairs, kt
        self.pair0, self.unit0, self.load0 = pair0, unit0, load0
        self.drained0, self.gate0, self.hid0 = drained0, gate0, hid0
        self.drains = 1 if name == "in" else 2
        self.used0 = unit0 - pair0
        self.upp = -(-kt // K_UNIT)
        self.units = pairs * self.upp
        self.loads = self.units // 2

    def k_of(self, v):
        a = v % self.upp * K_UNIT
        return range(a, min(a + K_UNIT, self.kt))


GAIN_OF = {0: 0, 3: 2, 5: 3, 7: 4, 9: 5, 11: 6}
NEW_NORM = (0, 3, 5, 9, 11)
RB_COUNT = (1, 3, 4, 5, 6)
X_WITHIN = {4: 5, 8: 9}
X_AFTER = {2: 3, 6: 7, 10: 11}


def plan():
    out, pair, unit, drained, gates, hids = [], 0, 0, 0, 0, 0
    for name, pairs, kt in PHASES:
        p = Phase(name, pairs, kt, pair, unit, unit // 2, drained, gates, hids)
        out.append(p)
        pair, unit, drained = pair + p.pairs, unit + p.units, drained + p.pairs * p.drains
        gates += pairs if name in ("in", "glu") else 0
        hids += pairs if name == "in" else 0
        assert p.units % SPLIT_SLOTS == 0 and p.pairs % PAIR_BANKS == 0
    return out


def unit_done(p, v):
    j, n = divmod(v, p.upp)
    if n == p.upp - 1:
        return True, p.pair0 + j + 1
    return False, p.used0 + j * (p.upp - 1) + n + 1


def free_at(phases, gp):
    p = [p for p in phases if p.pair0 <= gp][-1]
    return p.drained0 + (gp - p.pair0) * p.drains + (1 if p.name == "glu" else p.drains)


def trunk(nc, io, out):
    phases = plan()
    all_units = [(p, v) for p in phases for v in range(p.units)]

    ctx = ExitStack()

    def sb(name, shape, dt=F32, where=None):
        return (where or ctx).enter_context(nc.sbuf_tensor(name, shape, dt))

    def sem(name):
        return ctx.enter_context(nc.semaphore(name))

    with ctx:
        raw = sb("raw", [P, RAW_SLOTS, 2 * UW])
        w_hi = sb("w_hi", [P, SPLIT_SLOTS, UW], F32R)
        w_lo = sb("w_lo", [P, SPLIT_SLOTS, UW], F32R)
        x_hi = sb("x_hi", [P, DT, TOK], F32R)
        x_lo = sb("x_lo", [P, DT, TOK], F32R)
        h = sb("h", [P, DT, TOK])
        ident = sb("ident", [P, P])
        ones = sb("ones", [P, P])
        gate = sb("gate", [P, 2, TOK])
        prod = sb("prod", [P, 2, TOK])
        rb = sb("rb", [P, TOK])
        sq = sb("sq", [P, 2, TOK])
        gains = sb("gains", [P, NORMS, DT])
        skip = sb("skip", [P, DT])
        ms = sb("ms", [P, TT])
        mhalf = sb("mhalf", [P, TT])
        rs = sb("rs", [P, TT])
        half = sb("half", [P, 2])
        diag = sb("diag", [P, TT, P])
        with ExitStack() as area:
            w2_bd = sb("w2_bd", [P, 2, 2, STEP, PPT, 32], F32, area)
            c_bd = sb("c_bd", [P, 3, 2, PPT, STEP + 1, 32], F32, area)
            decay = sb("decay", [P, 2, PPT, CH], F32, area)
            um = sb("um", [P, PPT, TOK], F32, area)
            w2_t = sb("w2_t", [P, 2, 2, STEP, P], F32, area)
            k_t = sb("k_t", [P, 2, STEP, 32], F32, area)
            rot_a = sb("rot_a", [P, 2, PPT, CH], F32, area)
            rot_b = sb("rot_b", [P, 2, PPT, CH], F32, area)
        y, z = sq, prod
        hid_hi = sb("hid_hi", [P, FT, TOK], F32R)
        hid_lo = sb("hid_lo", [P, FT, TOK], F32R)
        with ExitStack() as area:
            w2 = sb("w2", [P, 2, STEP, GP, S5_J], F32, area)
            cp = sb("cp", [P, 2, GP, STEP + 1, S5_J], F32, area)
            rotc = sb("rotc", [P, GP, CH], F32, area)
            rots = sb("rots", [P, GP, CH], F32, area)
            sm = sb("sm", [P, SMALLS, GP], F32, area)
            with ExitStack() as inner:
                tmp = sb("tmp", [P, 4, GP * S5_J], F32, inner)
            rot_in = sb("rot_in", [P, 2, PPT, CH], F32, area)
            scan = sb("scan", [P, 2, PPT, CH], F32, area)
            states = sb("states", [P, 2, 2, PPT, CH], F32, area)
            u = sb("u", [P, 3, TOK], F32, area)
        k_sb = sb("k_sb", [P, DT, TOK])
        v_sb = sb("v_sb", [P, TT, D])
        q_sb = sb("q_sb", [P, DT, TOK])
        dist = sb("dist", [P, P + TOK])
        sc = sb("sc", [P, 2, P + TOK])
        pr = sb("pr", [P, 3, P + TOK])
        pt = sb("pt", [P, 2, TOK + P])
        mx = sb("mx", [P, HEADS, 2, TT])
        sums = sb("sums", [P, HEADS, 2, TT])

        ps = ctx.enter_context(nc.psum_tensor("ps", [P, 8, 512], F32))
        SS, RB, TA, TB = 4, 5, 6, 7

        landed = [sem(f"landed{i}") for i in range(RAW_SLOTS)]
        hi_done = sem("hi_done")
        lo_done = sem("lo_done")
        unit_used = sem("unit_used")
        pair_done = sem("pair_done")
        drained = sem("drained")
        gate_ready = sem("gate_ready")
        hid_hi_done = sem("hid_hi_done")
        hid_ready = sem("hid_ready")
        x_in = [sem(f"x_in{c}") for c in range(DT // 2)]
        par_in = sem("par_in")
        s5_in = sem("s5_in")
        consts = sem("consts")
        sq_ready = sem("sq_ready")
        ss_done = sem("ss_done")
        ms_ready = sem("ms_ready")
        rs_ready = sem("rs_ready")
        diag_ready = sem("diag_ready")
        rb_ready = sem("rb_ready")
        rb_copied = sem("rb_copied")
        scaled = sem("scaled")
        x_hi_done = sem("x_hi_done")
        x_ready = sem("x_ready")
        s5_exp = sem("s5_exp")
        s5_small = sem("s5_small")
        pool_step = sem("pool_step")
        u_ready = sem("u_ready")
        um_zero = sem("um_zero")
        um_ready = sem("um_ready")
        bd_ready = sem("bd_ready")
        prep_done = sem("prep_done")
        prep_copied = sem("prep_copied")
        v_done = sem("v_done")
        dve_step = sem("dve_step")
        st_ready = sem("st_ready")
        y_done = sem("y_done")
        yf_ready = sem("yf_ready")
        z_ready = sem("z_ready")
        dist_ready = sem("dist_ready")
        s_done = sem("s_done")
        mx_ready = sem("mx_ready")
        exp_done = sem("exp_done")
        pr_ready = sem("pr_ready")
        t_done = sem("t_done")
        pt_ready = sem("pt_ready")
        o_done = sem("o_done")
        out_ready = sem("out_ready")
        out_sent = sem("out_sent")

        weights = [io[n] for n in ("in0", "out0", "glu", "in1", "out1", "k", "v", "in2", "out2",
                                   "q", "o", "in3", "out3")]

        made = {}
        block = ctx.enter_context(nc.Block())

        @block.sync
        def _(sp):
            def load_x(c):
                sp.dma_start(h[:, 2 * c:2 * c + 2, :], io["x"][:, 2 * c:2 * c + 2, :])\
                  .then_inc(x_in[c], 16)

            def load(n, c, i=0):
                p = phases[n]
                g = p.load0 + c
                if g >= RAW_SLOTS:
                    sp.wait_ge(lo_done, 2 * (g - RAW_SLOTS + 1) + 8 * i)
                per = p.upp // 2
                a = c % per * 2 * UW
                w = min(2 * UW, p.kt * 2 * P - a)
                src = weights[n][c // per + (4 * i if per == 1 else 0), :, a:a + w]
                sp.dma_start(raw[:, g % RAW_SLOTS, 0:w], src).then_inc(landed[g % RAW_SLOTS], 16)

            for n, p in enumerate(phases):
                if p.name == "in":
                    for c in range(4):
                        if n == 0:
                            load_x(c)
                        load(n, c)
                    with sp.Fori(0, p.loads // 4 - 1) as i:
                        for c in range(4, 8):
                            load(n, c, i)
                    for c in range(p.loads // 4 * 4, p.loads):
                        load(n, c)
                else:
                    for c in range(p.loads):
                        load(n, c)
            for d in range(DT):
                sp.wait_ge(out_ready, d + 1)
                sp.dma_start(out[:, d, :], h[:, d, :]).then_inc(out_sent, 16)
            sp.wait_ge(out_sent, 16 * DT)

        @block.gpsimd
        def _(pool):
            pool.memset(ident[:, :], 0.0).then_inc(pool_step, 1)
            pool.memset(mhalf[:, :], -0.5).then_inc(consts, 1)
            pool.memset(ones[:, :], 1.0).then_inc(consts, 1)
            pool.wait_ge(pool_step, 1)
            pool.affine_select(out=ident[:, :], in_=ident[:, :], compare_op=ALU.not_equal, fill=1.0,
                               base=0, pattern=[[-1, P]], channel_multiplier=1).then_inc(consts, 1)
            pool.memset(half[:, :], 1.0).then_inc(pool_step, 1)
            pool.wait_ge(pool_step, 2)
            pool.affine_select(out=half[:, 0:1], in_=half[:, 0:1], compare_op=ALU.is_ge, fill=0.0,
                               base=S5_N - 1, pattern=[[0, 1]], channel_multiplier=-1)\
                .then_inc(pool_step, 1)
            pool.affine_select(out=half[:, 1:2], in_=half[:, 1:2], compare_op=ALU.is_ge, fill=0.0,
                               base=-S5_N, pattern=[[0, 1]], channel_multiplier=1)\
                .then_inc(pool_step, 1)
            norms = [0]

            def inverse_rms():
                norms[0] += 1
                pool.wait_ge(ms_ready, norms[0])
                pool.tensor_tensor(rs[:, :], ms[:, :], mhalf[:, :], ALU.pow).then_inc(rs_ready, 1)

            steps = [4]

            def link(ins):
                ins.then_inc(pool_step, 1)
                steps[0] += 1
                pool.wait_ge(pool_step, steps[0])

            def tt(o, a, b, op):
                link(pool.tensor_tensor(o, a, b, op))

            def ts(o, a, s1, s2, op0=ALU.mult, op1=ALU.add):
                link(pool.tensor_scalar(o, a, s1, s2, op0, op1))

            (A_RE, A_IM, LS, DTM, XA, TH, KK, RR, COS, MAG, SIN, HALF, LR, LI, NR, DEN, FR, FI,
             T1, T2, PR, PI, QR, QI, MAG4, UR, UI) = range(27)

            def s(i):
                return sm[:, i, :]

            def cmul(o_r, o_i, a_r, a_i, b_r, b_i, t1, t2):
                tt(t1, a_r, b_r, ALU.mult)
                tt(t2, a_i, b_i, ALU.mult)
                tt(o_r, t1, t2, ALU.subtract)
                tt(t1, a_r, b_i, ALU.mult)
                tt(t2, a_i, b_r, ALU.mult)
                tt(o_i, t1, t2, ALU.add)

            pool.wait_ge(s5_in, 16 * S5_LOADS)
            ts(s(A_RE), s(A_RE), -1e-4, 0.0, ALU.min, ALU.add)
            pool.wait_ge(s5_exp, 1)
            tt(s(XA), s(A_RE), s(DTM), ALU.mult)
            tt(s(TH), s(A_IM), s(DTM), ALU.mult)
            ts(s(KK), s(TH), 1.0 / (2.0 * math.pi), ROUND)
            ts(s(KK), s(KK), -ROUND, 0.0, ALU.add, ALU.add)
            ts(s(T1), s(KK), -TWO_PI[0], 0.0)
            tt(s(RR), s(TH), s(T1), ALU.add)
            ts(s(T1), s(KK), -TWO_PI[1], 0.0)
            tt(s(RR), s(RR), s(T1), ALU.add)
            ts(s(T1), s(KK), -TWO_PI[2], 0.0)
            tt(s(RR), s(RR), s(T1), ALU.add)
            pool.tensor_scalar(s(RR), s(RR), PI_LOW, -PI_LOW, ALU.min, ALU.max)\
                .then_inc(s5_small, 1)
            pool.wait_ge(s5_exp, 4)
            inverse_rms()
            tt(s(COS), s(HALF), s(HALF), ALU.mult)
            ts(s(COS), s(COS), -2.0, 1.0)
            tt(s(LR), s(MAG), s(COS), ALU.mult)
            tt(s(LI), s(MAG), s(SIN), ALU.mult)
            ts(s(NR), s(LR), 1.0, -1.0)
            tt(s(T1), s(A_RE), s(A_RE), ALU.mult)
            tt(s(T2), s(A_IM), s(A_IM), ALU.mult)
            tt(s(DEN), s(T1), s(T2), ALU.add)
            tt(s(T1), s(NR), s(A_RE), ALU.mult)
            tt(s(T2), s(LI), s(A_IM), ALU.mult)
            tt(s(T1), s(T1), s(T2), ALU.add)
            link(pool.memset(s(T2), -1.0))
            tt(s(DEN), s(DEN), s(T2), ALU.pow)
            tt(s(FR), s(T1), s(DEN), ALU.mult)
            tt(s(T1), s(LI), s(A_RE), ALU.mult)
            tt(s(T2), s(NR), s(A_IM), ALU.mult)
            tt(s(T1), s(T1), s(T2), ALU.subtract)
            tt(s(FI), s(T1), s(DEN), ALU.mult)

            def wide(i):
                return s(i).unsqueeze(2).broadcast_to([P, GP, S5_J])

            def t(i):
                return tmp[:, i, :].rearrange("p (g j) -> p g j", j=S5_J)

            cmul(w2[:, 0, STEP - 1], w2[:, 1, STEP - 1], t(0), t(1), wide(FR), wide(FI), t(2), t(3))
            for k in range(STEP - 2, -1, -1):
                cmul(w2[:, 0, k], w2[:, 1, k], w2[:, 0, k + 1], w2[:, 1, k + 1], wide(LR), wide(LI),
                     t(2), t(3))
            for k in range(1, STEP + 1):
                cmul(cp[:, 0, :, k], cp[:, 1, :, k], cp[:, 0, :, k - 1], cp[:, 1, :, k - 1],
                     wide(LR), wide(LI), t(2), t(3))
            ts(cp[:, 1], cp[:, 1], -1.0, 0.0)
            tt(s(T1), s(MAG), s(MAG), ALU.mult)
            tt(s(MAG4), s(T1), s(T1), ALU.mult)
            cmul(s(PR), s(PI), s(COS), s(SIN), s(COS), s(SIN), s(T1), s(T2))
            cmul(s(UR), s(UI), s(PR), s(PI), s(PR), s(PI), s(T1), s(T2))
            link(pool.memset(rotc[:, :, 0:1], 1.0))
            link(pool.memset(rots[:, :, 0:1], 0.0))
            w, cur, nxt = 1, (UR, UI), (QR, QI)
            while w < CH:
                def b(i):
                    return s(i).unsqueeze(2).broadcast_to([P, GP, w])

                def part(k):
                    a = tmp[:, 2 * k:2 * k + 2, :].rearrange("p a x -> p (a x)")[:, 0:GP * w]
                    return a.rearrange("p (g c) -> p g c", c=w)

                cmul(rotc[:, :, w:2 * w], rots[:, :, w:2 * w], rotc[:, :, 0:w], rots[:, :, 0:w],
                     b(cur[0]), b(cur[1]), part(0), part(1))
                cmul(s(nxt[0]), s(nxt[1]), s(cur[0]), s(cur[1]), s(cur[0]), s(cur[1]), s(T1), s(T2))
                w, cur, nxt = 2 * w, nxt, cur
            made["s5"] = steps[0]
            inverse_rms()

            pool.memset(um[:, :, :], 0.0).then_inc(um_zero, 1)
            for d in range(DT):
                b = d % 2
                if d >= 2:
                    pool.wait_ge(prep_done, d - 1)
                for g in range(2):
                    cols = slice(S5_J * g, S5_J * g + S5_J)
                    for r in range(2):
                        pool.tensor_scalar(w2_bd[:, b, r, :, :, cols],
                                           w2[:, r, :, PPT * d:PPT * d + PPT, :],
                                           half[:, g:g + 1], 0.0,
                                           ALU.mult, ALU.add).then_inc(bd_ready, 1)
                if d >= 3:
                    pool.wait_ge(y_done, d - 2)
                for g in range(2):
                    cols = slice(S5_J * g, S5_J * g + S5_J)
                    for r in range(2):
                        pool.tensor_scalar(c_bd[:, d % 3, r, :, :, cols],
                                           cp[:, r, PPT * d:PPT * d + PPT, :, :],
                                           half[:, g:g + 1], 0.0,
                                           ALU.mult, ALU.add).then_inc(bd_ready, 1)
                if d >= 2:
                    pool.wait_ge(st_ready, 2 * (d - 1))
                pool.tensor_scalar(decay[:, b, :, 1:CH],
                                   s(MAG4)[:, PPT * d:PPT * d + PPT].unsqueeze(2)
                                   .broadcast_to([P, PPT, CH - 1]),
                                   1.0, 0.0, ALU.mult, ALU.add).then_inc(bd_ready, 1)
                pool.memset(decay[:, b, :, 0:1], 0.0).then_inc(bd_ready, 1)
            for _ in range(2):
                inverse_rms()
            for q0, c0, w in ((0, 0, P), (P, P, TOK)):
                part = dist[:, c0:c0 + w]
                pool.iota(part, [[1, w]], base=-q0, channel_multiplier=-1,
                          allow_small_or_imprecise_dtypes=True).then_inc(dist_ready, 1)
            pool.wait_ge(dist_ready, 2)
            for q0, c0, w in ((0, 0, P), (P, P, TOK)):
                part = dist[:, c0:c0 + w]
                pool.affine_select(out=part, in_=part, compare_op=ALU.is_ge, fill=NEG, base=q0,
                                   pattern=[[-1, w]], channel_multiplier=1).then_inc(dist_ready, 1)
            for _ in range(3):
                inverse_rms()

        @block.scalar
        def _(act):
            act.dma_start(gains[:, :, :], io["gains"]).then_inc(par_in, 16)
            act.dma_start(skip[:, :], io["skip"]).then_inc(par_in, 16)
            act.dma_start(sm[:, 0, :], io["a_re"]).then_inc(s5_in, 16)
            act.dma_start(sm[:, 1, :], io["a_im"]).then_inc(s5_in, 16)
            for g in range(2):
                act.dma_start(sm[64 * g:64 * g + 64, 2, :],
                              io["log_step"][g:g + 1, :].broadcast_to([64, GP])).then_inc(s5_in, 16)
            act.dma_start(tmp[:, 0, :], io["b_re"]).then_inc(s5_in, 16)
            act.dma_start(tmp[:, 1, :], io["b_im"]).then_inc(s5_in, 16)
            act.dma_start(cp[:, 0, :, 0, :], io["c_re"].rearrange("p (g j) -> p g j", j=S5_J)).then_inc(s5_in, 16)
            act.dma_start(cp[:, 1, :, 0, :], io["c_im"].rearrange("p (g j) -> p g j", j=S5_J)).then_inc(s5_in, 16)

            def split(gu, i=0):
                if gu >= len(all_units):
                    return
                p, v = all_units[gu]
                ld = gu // 2
                w = len(p.k_of(v)) * 2 * P
                if gu % 2 == 0:
                    act.wait_ge(landed[ld % RAW_SLOTS], 16 * (ld // RAW_SLOTS + 1) + 16 * i)
                if gu >= SPLIT_SLOTS:
                    last, value = unit_done(*all_units[gu - SPLIT_SLOTS])
                    act.wait_ge(pair_done if last else unit_used, value + 4 * i)
                a = gu % 2 * UW
                act.activation(w_hi[:, gu % SPLIT_SLOTS, 0:w], raw[:, ld % RAW_SLOTS, a:a + w],
                               ACT.Copy).then_inc(hi_done, 1)

            def square(d, ready, count):
                act.wait_ge(drained, ready)
                if count >= 2:
                    act.wait_ge(ss_done, count - 1)
                act.activation(sq[:, count % 2, :], h[:, d, :], ACT.Square).then_inc(sq_ready, 1)

            def high_x(d, n):
                act.activation(x_hi[:, d, :], h[:, d, :], ACT.Copy,
                               scale=gains[:, GAIN_OF[n], d:d + 1]).then_inc(x_hi_done, 1)

            tally = {"sq": 0, "rb": 0}

            def squares(tiles, ready):
                for n, d in enumerate(tiles):
                    square(d, ready + n, tally["sq"])
                    tally["sq"] += 1

            def copy_rb():
                tally["rb"] += 1
                act.wait_ge(rb_ready, RB_COUNT[tally["rb"] - 1])
                act.activation(rb[:, :], ps[:, RB, 0:TOK], ACT.Copy).then_inc(rb_copied, 1)

            def drain(n, p, j, i=0):
                gp = p.pair0 + j
                if p.name == "in":
                    act.wait_ge(scaled, 2 * (p.hid0 + j) + 1 + 8 * i)
                    act.activation(gate[:, 1, :], gate[:, 0, :], ACT.Silu).then_inc(gate_ready, 1)
                    act.wait_ge(drained, p.drained0 + j + 1 + 4 * i)
                    act.activation(hid_hi[:, j + 4 * i, :], prod[:, gp % 2, :], ACT.Copy)\
                       .then_inc(hid_hi_done, 1)
                elif p.name == "glu":
                    act.wait_ge(pair_done, gp + 1)
                    act.activation(gate[:, 1, :], ps[:, 2 * (gp % 2) + 1, 0:TOK], ACT.Sigmoid)\
                       .then_inc(gate_ready, 1)
                    if j < DT - 1:
                        squares([j], p.drained0 + 2 * j + 2)
                elif p.name in ("out", "o"):
                    if n in X_WITHIN:
                        for m in range(2):
                            act.wait_ge(drained, p.drained0 + 2 * j + m + 1)
                            high_x(2 * j + m, X_WITHIN[n])
                    if n != 10 or j < p.pairs - 1:
                        squares([2 * j, 2 * j + 1], p.drained0 + 2 * j + 1)

            def phase(n):
                p = phases[n]

                def step(v, i=0):
                    split(p.unit0 + v + LEAD, i)
                    if v == 1 and n in NEW_NORM:
                        copy_rb()
                    if v % p.upp == p.upp - 1:
                        drain(n, p, v // p.upp, i)

                if p.name == "in":
                    for v in range(8):
                        step(v)
                    with act.Fori(0, p.units // 8 - 1) as i:
                        for v in range(8, 16):
                            step(v, i)
                    for v in range(p.units // 8 * 8, p.units):
                        step(v)
                else:
                    for v in range(p.units):
                        step(v)
                if n in X_AFTER:
                    act.wait_ge(pair_done, p.pair0 + p.pairs)
                    for d in range(DT):
                        if n != 6:
                            act.wait_ge(drained, p.drained0 + 2 * p.pairs - (DT - 1 - d)
                                        * (2 if n == 2 else 1))
                        high_x(d, X_AFTER[n])
                    if n == 2:
                        squares([DT - 1], p.drained0 + 2 * p.pairs)
                    if n == 10:
                        squares([DT - 2, DT - 1], p.drained0 + 2 * p.pairs - 1)

            act.wait_ge(par_in, 32)
            for d in range(DT):
                if d % 2 == 0:
                    act.wait_ge(x_in[d // 2], 16)
                high_x(d, 0)
                if d == 1:
                    split(0)
                if d == 3:
                    split(1)
            for d in range(DT):
                if d >= 2:
                    act.wait_ge(ss_done, d - 1)
                act.activation(sq[:, d % 2, :], h[:, d, :], ACT.Square).then_inc(sq_ready, 1)
            tally["sq"] = DT
            act.wait_ge(s5_in, 16 * S5_LOADS)
            act.activation(sm[:, 3, :], sm[:, 2, :], ACT.Exp).then_inc(s5_exp, 1)
            act.wait_ge(s5_small, 1)
            act.activation(sm[:, 9, :], sm[:, 4, :], ACT.Exp).then_inc(s5_exp, 1)
            act.activation(sm[:, 10, :], sm[:, 7, :], ACT.Sin).then_inc(s5_exp, 1)
            act.activation(sm[:, 11, :], sm[:, 7, :], ACT.Sin, scale=0.5).then_inc(s5_exp, 1)
            phase(0)
            phase(1)

            def prep_copy(d):
                act.wait_ge(prep_done, d + 1)
                if d >= 2:
                    act.wait_ge(v_done, d - 1)
                for r, bank in ((0, TA), (1, TB)):
                    act.activation(w2_t[:, d % 2, r, :, :].rearrange("p s x -> p (s x)"), ps[:, bank, :],
                                   ACT.Copy).then_inc(prep_copied, 1)
                if d >= 2:
                    act.wait_ge(y_done, d - 1)
                act.activation(k_t[:, d % 2, :, :].rearrange("p s x -> p (s x)"),
                               ps[:, SS, 0:P], ACT.Copy).then_inc(prep_copied, 1)

            def gelu(d):
                act.wait_ge(yf_ready, d + 1)
                if d >= 2:
                    act.wait_ge(x_ready, DT + d - 1)
                act.activation(z[:, d % 2, :], y[:, d % 2, :], ACT.Gelu_apprx_tanh)\
                   .then_inc(z_ready, 1)
                act.wait_ge(z_ready, d + 1)
                act.activation(x_hi[:, d, :], z[:, d % 2, :], ACT.Copy).then_inc(x_hi_done, 1)

            def part_pairs(d):
                act.wait_ge(u_ready, d + 1)
                if d == 0:
                    act.wait_ge(um_zero, 1)
                if d >= 1:
                    act.wait_ge(v_done, d)
                for g in range(PPT):
                    rows = slice(32 * g, 32 * g + 32)
                    act.activation(um[rows, g, :], u[rows, d % 3, :], ACT.Copy)\
                       .then_inc(um_ready, 1)

            part_pairs(0)
            prep_copy(0)
            prep_copy(1)
            part_pairs(1)
            for d in range(DT):
                if d + 2 < DT:
                    part_pairs(d + 2)
                    prep_copy(d + 2)
                if d >= 1:
                    gelu(d - 1)
            gelu(DT - 1)
            for n in range(2, 10):
                phase(n)

            def exps(n):
                act.wait_ge(mx_ready, n + 1)
                if n >= 3:
                    act.wait_ge(t_done, n - 2)
                for q, a, w in ((0, 0, P), (1, P, TOK)):
                    act.activation(pr[:, n % 3, a:a + w], sc[:, n % 2, a:a + w], ACT.Exp,
                                   bias=mx[:, n, 1, q:q + 1],
                                   accum_out=sums[:, n, 0, q:q + 1]).then_inc(exp_done, 1)

            def pt_copy(n):
                act.wait_ge(t_done, n + 1)
                if n >= 2:
                    act.wait_ge(o_done, n - 1)
                act.activation(pt[:, n % 2, :], ps[:, 2 + n % 2, 0:TOK + P], ACT.Copy)\
                   .then_inc(pt_ready, 1)

            def high_o(n):
                act.wait_ge(o_done, n + 1)
                act.activation(x_hi[:, n // 2, :], ps[:, 6 + n // 2 % 2, 0:TOK], ACT.Copy)\
                   .then_inc(x_hi_done, 1)

            for n in range(HEADS + 4):
                if n < HEADS:
                    exps(n)
                if 2 <= n < HEADS + 2:
                    pt_copy(n - 2)
                if n >= 4 and (n - 4) % 2 == 1:
                    high_o(n - 4)
            phase(10)
            phase(11)
            phase(12)

        @block.vector
        def _(dve):
            tally = {"xf": 0, "x": 0, "norm": 0, "step": 0}

            def link(ins):
                ins.then_inc(dve_step, 1)
                tally["step"] += 1
                dve.wait_ge(dve_step, tally["step"])

            def split(gu, i=0):
                if gu >= len(all_units):
                    return
                p, v = all_units[gu]
                w = len(p.k_of(v)) * 2 * P
                a = gu % 2 * UW
                dve.wait_ge(hi_done, gu + 1 + 8 * i)
                dve.tensor_tensor(w_lo[:, gu % SPLIT_SLOTS, 0:w],
                                  raw[:, gu // 2 % RAW_SLOTS, a:a + w],
                                  w_hi[:, gu % SPLIT_SLOTS, 0:w].bitcast(F32),
                                  ALU.subtract).then_inc(lo_done, 1)

            def low_x(src):
                dve.wait_ge(x_hi_done, tally["x"] + 1)
                d = tally["x"] % DT
                dve.tensor_tensor(x_lo[:, d, :], src, x_hi[:, d, :].bitcast(F32), ALU.subtract)\
                   .then_inc(x_ready, 1)
                tally["x"] += 1

            def mean_squares():
                tally["norm"] += 1
                dve.wait_ge(ss_done, DT * tally["norm"])
                dve.tensor_scalar(ms[:, :], ps[:, SS, 0:TT], 1.0 / D, EPS, ALU.mult, ALU.add)\
                   .then_inc(ms_ready, 1)

            def diagonals():
                dve.wait_ge(rs_ready, tally["norm"])
                dve.wait_ge(consts, 3)
                for q in range(TT):
                    dve.tensor_scalar(diag[:, q, :], ident[:, :], rs[:, q:q + 1], None, ALU.mult)\
                       .then_inc(diag_ready, 1)

            def rms():
                mean_squares()
                diagonals()
                dve.wait_ge(rb_ready, tally["norm"])

            def normed(dst, d, g):
                return dve.scalar_tensor_tensor(dst, h[:, d, :], gains[:, g, d:d + 1],
                                                ps[:, RB, 0:TOK], ALU.mult, ALU.mult)

            def low_h(n):
                dve.wait_ge(x_hi_done, tally["x"] + 1)
                d = tally["x"] % DT
                dve.scalar_tensor_tensor(x_lo[:, d, :], h[:, d, :], gains[:, GAIN_OF[n], d:d + 1],
                                         x_hi[:, d, :].bitcast(F32), ALU.mult, ALU.subtract)\
                   .then_inc(x_ready, 1)
                tally["x"] += 1

            def drain(n, p, j, i=0):
                gp = p.pair0 + j
                b = 2 * (gp % 2)
                if p.name == "in":
                    dve.wait_ge(pair_done, gp + 1 + 4 * i)
                    dve.tensor_tensor(gate[:, 0, :], ps[:, b, 0:TOK], rb[:, :], ALU.mult)\
                       .then_inc(scaled, 1)
                    dve.wait_ge(gate_ready, p.gate0 + j + 1 + 4 * i)
                    dve.tensor_tensor(gate[:, 0, :], gate[:, 1, :], rb[:, :], ALU.mult)\
                       .then_inc(scaled, 1)
                    dve.wait_ge(scaled, 2 * (p.hid0 + j + 1) + 8 * i)
                    dve.tensor_tensor(prod[:, gp % 2, :], gate[:, 0, :], ps[:, b + 1, 0:TOK], ALU.mult)\
                       .then_inc(drained, 1)
                    dve.wait_ge(hid_hi_done, p.hid0 + j + 1 + 4 * i)
                    dve.tensor_tensor(hid_lo[:, j + 4 * i, :], prod[:, gp % 2, :],
                                      hid_hi[:, j + 4 * i, :].bitcast(F32), ALU.subtract)\
                       .then_inc(hid_ready, 1)
                    return
                if p.name == "glu":
                    dve.wait_ge(gate_ready, p.gate0 + j + 1)
                    dve.tensor_tensor(prod[:, gp % 2, :], gate[:, 1, :], ps[:, b, 0:TOK], ALU.mult)\
                       .then_inc(drained, 1)
                    dve.wait_ge(drained, p.drained0 + 2 * j + 1)
                    dve.tensor_tensor(h[:, j, :], h[:, j, :], prod[:, gp % 2, :], ALU.add)\
                       .then_inc(drained, 1)
                    return
                dve.wait_ge(pair_done, gp + 1)
                for m in range(2):
                    src = ps[:, b + m, 0:TOK]
                    d = 2 * j + m
                    if p.name in ("out", "o"):
                        ins = dve.scalar_tensor_tensor(h[:, d, :], src,
                                                       0.5 if p.name == "out" else 1.0,
                                                       h[:, d, :], ALU.mult, ALU.add)
                    elif p.name == "k":
                        ins = dve.tensor_tensor(k_sb[:, d, :], src, rb[:, :], ALU.mult)
                    elif p.name == "v":
                        ins = dve.tensor_scalar(v_sb[:, m, 2 * P * j:2 * P * j + 2 * P], src,
                                                rs[:, m:m + 1], None, ALU.mult)
                    else:
                        ins = dve.scalar_tensor_tensor(q_sb[:, d, :], src, HD ** -0.5, rb[:, :],
                                                       ALU.mult, ALU.mult)
                    ins.then_inc(drained, 1)
                if n in X_WITHIN:
                    low_h(X_WITHIN[n])
                    low_h(X_WITHIN[n])

            def phase(n):
                p = phases[n]

                def step(v, i=0):
                    split(p.unit0 + v + LEAD, i)
                    if v == 0 and n in NEW_NORM:
                        mean_squares()
                    if v == 1 and n in NEW_NORM:
                        diagonals()
                        dve.wait_ge(rb_copied, NEW_NORM.index(n) + 1)
                    if v % p.upp == p.upp - 1:
                        drain(n, p, v // p.upp, i)

                if p.name == "in":
                    for v in range(8):
                        step(v)
                    with dve.Fori(0, p.units // 8 - 1) as i:
                        for v in range(8, 16):
                            step(v, i)
                    for v in range(p.units // 8 * 8, p.units):
                        step(v)
                else:
                    for v in range(p.units):
                        step(v)
                if n in X_AFTER:
                    for d in range(DT):
                        low_h(X_AFTER[n])

            for d in range(DT):
                low_h(0)
                if d == 1:
                    split(0)
                if d == 3:
                    split(1)
            phase(0)
            phase(1)

            rms()
            dve.wait_ge(pool_step, made["s5"])

            def mixer_input(d):
                if d >= 3:
                    dve.wait_ge(um_ready, PPT * (d - 2))
                    dve.wait_ge(yf_ready, d - 2)
                normed(u[:, d % 3, :], d, 1).then_inc(u_ready, 1)

            def turn(dst_r, dst_i, src_r, src_i, d, back):
                g = slice(PPT * d, PPT * d + PPT)
                cs, sn = rotc[:, g, :], rots[:, g, :]
                dve.tensor_tensor(rot_a[:, 0], src_r, cs, ALU.mult).then_inc(dve_step, 1)
                dve.tensor_tensor(rot_b[:, 0], src_i, sn, ALU.mult).then_inc(dve_step, 1)
                dve.tensor_tensor(rot_a[:, 1], src_i, cs, ALU.mult).then_inc(dve_step, 1)
                dve.tensor_tensor(rot_b[:, 1], src_r, sn, ALU.mult).then_inc(dve_step, 1)
                tally["step"] += 4
                dve.wait_ge(dve_step, tally["step"])
                plus, minus = (ALU.subtract, ALU.add) if back else (ALU.add, ALU.subtract)
                return (dve.tensor_tensor(dst_r, rot_a[:, 0], rot_b[:, 0], plus),
                        dve.tensor_tensor(dst_i, rot_a[:, 1], rot_b[:, 1], minus))

            def scan_tile(d):
                b = d % 2
                v = ps[:, b, :].rearrange("p (r g c) -> p r g c", r=2, c=CH)
                dve.wait_ge(v_done, d + 1)
                for ins in turn(rot_in[:, 0], rot_in[:, 1], v[:, 0], v[:, 1], d, False):
                    ins.then_inc(dve_step, 1)
                tally["step"] += 2
                dve.wait_ge(dve_step, tally["step"])
                dve.wait_ge(bd_ready, BD_STEPS * (d + 1))
                for r in range(2):
                    dve.tensor_tensor_scan(scan[:, r].rearrange("p g c -> p (g c)"),
                                           decay[:, b].rearrange("p g c -> p (g c)"),
                                           rot_in[:, r].rearrange("p g c -> p (g c)"),
                                           0.0, ALU.mult, ALU.add).then_inc(dve_step, 1)
                tally["step"] += 2
                dve.wait_ge(dve_step, tally["step"])
                if d >= 2:
                    dve.wait_ge(y_done, d - 1)
                for ins in turn(states[:, b, 0], states[:, b, 1], scan[:, 0], scan[:, 1], d, True):
                    ins.then_inc(st_ready, 1)

            def add_skip(d):
                dve.wait_ge(y_done, d + 1)
                if d >= 2:
                    dve.wait_ge(z_ready, d - 1)
                dve.scalar_tensor_tensor(y[:, d % 2, :], u[:, d % 3, :], skip[:, d:d + 1],
                                         ps[:, 2 + d % 2, 0:TOK], ALU.mult, ALU.add)\
                   .then_inc(yf_ready, 1)

            mixer_input(0)
            mixer_input(1)
            for d in range(DT + 2):
                if d < DT:
                    if d >= 1:
                        dve.wait_ge(st_ready, 2 * d)
                    scan_tile(d)
                if 1 <= d <= DT:
                    add_skip(d - 1)
                if d + 2 < DT:
                    mixer_input(d + 2)
                if d >= 2:
                    low_x(z[:, d % 2, :])
            for n in range(2, 10):
                phase(n)

            dve.wait_ge(dist_ready, 4)

            def shifted_max(n):
                b = n % 2
                dve.wait_ge(s_done, n + 1)
                if n >= 2:
                    dve.wait_ge(exp_done, 2 * (n - 1))
                slope = 2.0 ** (-8.0 * (n + 1) / HEADS)
                link(dve.scalar_tensor_tensor(sc[:, b, :], dist[:, :], slope,
                                              ps[:, b, 0:P + TOK], ALU.mult, ALU.add))
                for q, a, w in ((0, 0, P), (1, P, TOK)):
                    ins = dve.reduce_max(mx[:, n, 0, q:q + 1], sc[:, b, a:a + w], AX_X)
                    ins.then_inc(dve_step, 1)
                tally["step"] += 2
                dve.wait_ge(dve_step, tally["step"])
                dve.tensor_scalar(mx[:, n, 1, :], mx[:, n, 0, :], -1.0, None, ALU.mult)\
                   .then_inc(mx_ready, 1)

            def normalise(n):
                dve.wait_ge(exp_done, 2 * (n + 1))
                link(dve.reciprocal(sums[:, n, 1, :], sums[:, n, 0, :]))
                for q, a, w in ((0, 0, P), (1, P, TOK)):
                    dve.tensor_scalar(pr[:, n % 3, a:a + w], pr[:, n % 3, a:a + w],
                                      sums[:, n, 1, q:q + 1], None, ALU.mult).then_inc(pr_ready, 1)

            for n in range(HEADS + 4):
                if n < HEADS:
                    shifted_max(n)
                if 1 <= n <= HEADS:
                    normalise(n - 1)
                if n >= 4 and (n - 4) % 2 == 1:
                    low_x(ps[:, 6 + (n - 4) // 2 % 2, 0:TOK])
            phase(10)
            phase(11)
            phase(12)
            rms()
            for d in range(DT):
                normed(h[:, d, :], d, 7).then_inc(out_ready, 1)

        @block.tensor
        def _(pe):
            tally = {"sq": 0, "norm": 0, "x": 0}

            def mm(o, w, x, start, stop, **kw):
                return pe.matmul(o, w, x, start=start, stop=stop, skip_group_check=True, **kw)

            def sum_squares(tiles):
                for d in tiles:
                    k = tally["sq"]
                    pe.wait_ge(sq_ready, k + 1)
                    if k == 0:
                        pe.wait_ge(consts, 3)
                    for q in range(TT):
                        last = mm(ps[:, SS, q:q + 1], sq[:, k % 2, q * P:q * P + P], ones[:, 0:1],
                                  d == 0 and q == 0, d == DT - 1)
                    last.then_inc(ss_done, 1)
                    tally["sq"] += 1

            def broadcast():
                tally["norm"] += 1
                pe.wait_ge(diag_ready, TT * tally["norm"])
                for q in range(TT):
                    last = mm(ps[:, RB, q * P:q * P + P], ones[:, :], diag[:, q, :], True, True)
                last.then_inc(rb_ready, 1)

            def pair(p, j, i=0, first=False, late=()):
                gp = p.pair0 + j
                if gp >= PAIR_BANKS:
                    pe.wait_ge(drained, free_at(phases, gp - PAIR_BANKS) + p.drains * 2 * i)
                b = 2 * (gp % 2)
                hi, lo = (hid_hi, hid_lo) if p.name == "out" else (x_hi, x_lo)
                for n in range(p.upp):
                    gu = p.unit0 + j * p.upp + n
                    s = gu % SPLIT_SLOTS
                    pe.wait_ge(lo_done, gu + 1 + 2 * p.upp * i)
                    for k in p.k_of(n):
                        if first:
                            if p.name == "out":
                                pe.wait_ge(hid_ready, p.hid0 - FT + k + 1)
                            else:
                                pe.wait_ge(x_ready, tally["x"] + k + 1)
                        st, sp_ = k == 0, k == p.kt - 1
                        a = (k - n * K_UNIT) * 2 * P
                        for m in range(2):
                            o = ps[:, b + m, 0:TOK]
                            if p.name == "v":
                                tok = slice(m * P, m * P + P)
                                mm(o, hi[:, k, tok], w_hi[:, s, a:a + 2 * P], st, False)
                                mm(o, hi[:, k, tok], w_lo[:, s, a:a + 2 * P], False, False)
                                last = mm(o, lo[:, k, tok], w_hi[:, s, a:a + 2 * P], False, sp_)
                            else:
                                w = slice(a + m * P, a + m * P + P)
                                mm(o, w_hi[:, s, w], hi[:, k, :], st, False)
                                mm(o, w_hi[:, s, w], lo[:, k, :], False, False)
                                last = mm(o, w_lo[:, s, w], hi[:, k, :], False, sp_)
                    if n < p.upp - 1:
                        last.then_inc(unit_used, 1)
                        if n == 0 and late:
                            sum_squares(late)
                last.then_inc(pair_done, 1)

            def phase(n):
                p = phases[n]
                late = {0: range(DT), 3: [DT - 1], 5: [DT - 2, DT - 1], 9: [DT - 2, DT - 1],
                        11: [DT - 2, DT - 1]}.get(n, ())
                if p.name == "in":
                    pair(p, 0, first=True, late=late)
                    if n in NEW_NORM:
                        broadcast()
                    pair(p, 1)
                    with pe.Fori(0, p.pairs // 2 - 1) as i:
                        pair(p, 2, i)
                        pair(p, 3, i)
                else:
                    for j in range(p.pairs):
                        pair(p, j, first=j == 0 and p.name != "v", late=late if j == 0 else ())
                        if n in NEW_NORM and j == 0:
                            broadcast()
                        if p.name in ("out", "o") and j >= 1:
                            sum_squares([2 * j - 2, 2 * j - 1])
                        if p.name == "glu" and j >= 1:
                            sum_squares([j - 1])
                    if n in (1, 12):
                        sum_squares([DT - 2, DT - 1])
                if p.name not in ("out", "k"):
                    tally["x"] += DT

            phase(0)
            phase(1)
            broadcast()

            def prepare(d):
                b = d % 2
                pe.wait_ge(bd_ready, BD_STEPS * (d + 1))
                if d >= 1:
                    pe.wait_ge(prep_copied, 3 * d)
                for r, bank in ((0, TA), (1, TB)):
                    for t in range(STEP):
                        pe.transpose(ps[:, bank, t * P:t * P + P],
                                     w2_bd[:, b, r, t, :, :].rearrange("p g j -> p (g j)"),
                                     ident[:, :])
                for g in range(PPT):
                    rows = slice(32 * g, 32 * g + 32)
                    for r in range(2):
                        last = mm(ps[rows, SS, 0:P], w2_bd[:, b, r, STEP - 1, g, :],
                                  c_bd[:, d % 3, r, g, 0:STEP, :].rearrange("p t j -> p (t j)"),
                                  r == 0, r == 1)
                last.then_inc(prep_done, 1)

            def chunk_inputs(d):
                pe.wait_ge(prep_copied, 3 * (d + 1))
                pe.wait_ge(um_ready, PPT * (d + 1))
                if d >= 2:
                    pe.wait_ge(st_ready, 2 * (d - 1))
                us = um[:, :, :].rearrange("p g (c s) -> p s g c", s=STEP)
                for r in range(2):
                    a = r * PPT * CH
                    o = ps[:, d % 2, a:a + PPT * CH].rearrange("p (g c) -> p g c", c=CH)
                    for t in range(STEP):
                        last = mm(o, w2_t[:, d % 2, r, t, :], us[:, t, :, :], t == 0, t == STEP - 1)
                last.then_inc(v_done, 1)

            def outputs(d):
                b = d % 2
                if d >= 2:
                    pe.wait_ge(yf_ready, d - 1)
                uc = u[:, d % 3, :].rearrange("p (c s) -> p c s", s=STEP)
                yc = ps[:, 2 + b, 0:TOK].rearrange("p (c s) -> p c s", s=STEP)
                for g in range(PPT):
                    rows = slice(32 * g, 32 * g + 32)
                    for t in range(STEP):
                        mm(yc[rows, :, t:STEP], k_t[rows, b, t, :], uc[rows, :, 0:STEP - t],
                           t == 0, False)
                pe.wait_ge(st_ready, 2 * (d + 1))
                for g in range(PPT):
                    rows = slice(32 * g, 32 * g + 32)
                    for t in range(STEP):
                        for r in range(2):
                            last = mm(yc[rows, 1:CH, t], c_bd[:, d % 3, r, g, t + 1, :],
                                      states[:, b, r, g, 0:CH - 1], False, r == 1)
                last.then_inc(y_done, 1)

            prepare(0)
            chunk_inputs(0)
            prepare(1)
            for d in range(DT):
                if d + 1 < DT:
                    chunk_inputs(d + 1)
                if d + 2 < DT:
                    prepare(d + 2)
                outputs(d)
            for n in range(2, 10):
                phase(n)

            def scores(n):
                b, d = n % 2, n // 2
                rows = slice(HD * (n % 2), HD * (n % 2) + HD)
                if n == 0:
                    pe.wait_ge(drained, phases[10].drained0)
                if n >= 2:
                    pe.wait_ge(mx_ready, n - 1)
                for q, a, w in ((0, 0, P), (1, P, TOK)):
                    last = mm(ps[:, b, a:a + w], q_sb[rows, d, q * P:q * P + P], k_sb[rows, d, 0:w],
                              True, True)
                last.then_inc(s_done, 1)

            def turn_probs(n):
                pe.wait_ge(pr_ready, 2 * (n + 1))
                if n >= 2:
                    pe.wait_ge(pt_ready, n - 1)
                for a in range(3):
                    last = pe.transpose(ps[:, 2 + n % 2, a * P:a * P + P],
                                        pr[:, n % 3, a * P:a * P + P], ident[:, :])
                last.then_inc(t_done, 1)

            def head_output(n):
                bank = 6 + n // 2 % 2
                rows = slice(HD * (n % 2), HD * (n % 2) + HD)
                cols = slice(HD * n, HD * n + HD)
                pe.wait_ge(pt_ready, n + 1)
                if n >= 4:
                    pe.wait_ge(x_ready, tally["x"] + n // 2 - 1)
                mm(ps[rows, bank, 0:TOK], v_sb[:, 0, cols], pt[:, n % 2, 0:TOK], True, False)
                mm(ps[rows, bank, P:TOK], v_sb[:, 1, cols], pt[:, n % 2, TOK:TOK + P], False, True)\
                    .then_inc(o_done, 1)

            for n in range(HEADS + 3):
                if n < HEADS:
                    scores(n)
                if 2 <= n < HEADS + 2:
                    turn_probs(n - 2)
                if n >= 3:
                    head_output(n - 3)
            phase(10)
            phase(11)
            phase(12)
            broadcast()


def kernel(**inputs):
    import numpy as _np
    import concourse.bacc as _bacc
    from concourse import mybir as _mybir
    from concourse.bass_utils import run_bass_kernel_spmd as _run

    x = {k: _np.asarray(v) for k, v in inputs.items()}

    def pairs(w, halves):
        r, c = w.shape
        if halves:
            w = w.reshape(r // P, P, 2, c // (2 * P), P).transpose(3, 1, 0, 2, 4)
        else:
            w = w.reshape(r // P, P, c // (2 * P), 2, P).transpose(2, 1, 0, 3, 4)
        return _np.ascontiguousarray(w.reshape(w.shape[0], P, -1))

    def tiles(v):
        return _np.ascontiguousarray(_np.moveaxis(v.reshape(v.shape[:-1] + (DT, P)), -1, 0))

    def states(v):
        v = v.reshape((GP, 2 * S5_N) + v.shape[2:])
        return _np.ascontiguousarray(_np.moveaxis(v, 1, 0).reshape(P, -1))

    arrays = {
        "x": _np.ascontiguousarray(x["x"][0].T.reshape(DT, P, TOK).transpose(1, 0, 2)),
        "gains": tiles(_np.stack([x["ffn1_norm"][0], x["mix_norm"][0], x["ffn2_norm"][0],
                                  x["kv_norm"], x["ffn1_norm"][1], x["mix_norm"][1],
                                  x["ffn2_norm"][1], x["final_norm"]])),
        "skip": tiles(x["s5_d"][0]),
        "a_re": states(x["s5_a_re"][0]), "a_im": states(x["s5_a_im"][0]),
        "log_step": _np.ascontiguousarray(x["s5_log_step"][0].reshape(GP, 2).T),
        "b_re": states(x["s5_b_re"][0]), "b_im": states(x["s5_b_im"][0]),
        "c_re": states(x["s5_c_re"][0].transpose(0, 2, 1)),
        "c_im": states(x["s5_c_im"][0].transpose(0, 2, 1)),
        "glu": pairs(x["s5_w_glu"][0], True),
        "k": pairs(x["w_kv"][:, :D], False), "v": pairs(x["w_kv"][:, D:], False),
        "q": pairs(x["w_q"][0], False), "o": pairs(x["w_o"][0], False),
    }
    for n, (layer, ffn) in enumerate(((0, 1), (0, 2), (1, 1), (1, 2))):
        arrays[f"in{n}"] = pairs(x[f"ffn{ffn}_w_in"][layer], True)
        arrays[f"out{n}"] = pairs(x[f"ffn{ffn}_w_out"][layer], False)

    nc = _bacc.Bacc("TRN2", target_bir_lowering=False, num_devices=1)
    io = {k: nc.dram_tensor(f"in_{k}", a.shape, _mybir.dt.from_np(a.dtype), kind="ExternalInput").ap()
          for k, a in arrays.items()}
    out = nc.dram_tensor("out_x", (P, DT, TOK), F32, kind="ExternalOutput").ap()
    trunk(nc, io, out)
    r = _run(nc, [{f"in_{k}": a for k, a in arrays.items()}], core_ids=[0])
    got = r.results[0]["out_x"]
    return _np.ascontiguousarray(got.transpose(2, 1, 0).reshape(1, TOK, D))
```
